# Optimizing a Trainium2 kernel written in Bass

```python
import math
import jax, jax.numpy as jnp
from jax import lax
import numpy as np

D_MODEL = 2048
BATCH = 1
SEQ = 512
DEPTH = 2
DEC_BATCH = 8
DEC_SEQ = 4
PAST_LEN = 2048
PAGE_SIZE = 128

N_HEADS = 8
HEAD_DIM = 128
N_KV_HEADS = 2
ATT_W = N_HEADS * HEAD_DIM
KV_W = N_KV_HEADS * HEAD_DIM
N_IDX_HEADS = 16
IDX_DIM = 64
TOPK_MAX = 256
CONV_W = D_MODEL // 2
CONV_K = 31
ROPE_THETA = 500000.0
QBLOCK = 128
EPS = 1e-6
IN_WIDTHS = (ATT_W, KV_W, KV_W, N_IDX_HEADS * IDX_DIM, IDX_DIM, N_IDX_HEADS, ATT_W, 2 * CONV_W, CONV_W, 2 * D_MODEL)
N_IN = sum(IN_WIDTHS)

kernel_name = 'dsa_conformer_gated_hybrid_step'

F32 = jnp.float32

def rms_norm(x, g):
    xf = x.astype(F32)
    y = xf * lax.rsqrt(jnp.mean(xf * xf, axis=-1, keepdims=True) + EPS)
    return (y * g.astype(F32)).astype(x.dtype)

def layer_norm(x, g, b):
    xf = x.astype(F32)
    mu = jnp.mean(xf, axis=-1, keepdims=True)
    xc = xf - mu
    y = xc * lax.rsqrt(jnp.mean(xc * xc, axis=-1, keepdims=True) + EPS)
    return (y * g.astype(F32) + b.astype(F32)).astype(x.dtype)

def rope(x, pos):
    rd = x.shape[-1] // 4
    half = rd // 2
    inv = ROPE_THETA ** (-jnp.arange(half, dtype=F32) / half)
    ang = pos.astype(F32)[:, None] * inv[None, :]
    cos = jnp.cos(ang)[:, None, :]
    sin = jnp.sin(ang)[:, None, :]
    xf = x.astype(F32)
    x1 = xf[..., :half]
    x2 = xf[..., half:rd]
    out = jnp.concatenate([x1 * cos - x2 * sin, x2 * cos + x1 * sin, xf[..., rd:]], axis=-1)
    return out.astype(x.dtype)

def split_in(z):
    offs = []
    acc = 0
    for w in IN_WIDTHS[:-1]:
        acc += w
        offs.append(acc)
    return jnp.split(z, offs, axis=-1)

def dsa_attend(q, qi, wi, k, v, ki, q_pos, top_k):
    b, t = q.shape[:2]
    n_keys = k.shape[1]
    dots = jnp.einsum('bthd,bsd->bths', qi.astype(F32), ki.astype(F32)) * (IDX_DIM ** -0.5)
    score = jnp.einsum('bths,bth->bts', jax.nn.relu(dots), wi.astype(F32))
    visible = jnp.arange(n_keys, dtype=jnp.int32)[None, :] <= q_pos[:, None]
    score = jnp.where(visible[None], score, -jnp.inf)
    _, idx = lax.top_k(score, top_k)
    valid = idx <= q_pos[None, :, None]
    take = jax.vmap(lambda rows, ids: rows[ids])
    kg = take(k, idx).astype(F32)
    vg = take(v, idx).astype(F32)
    qg = q.astype(F32).reshape(b, t, N_KV_HEADS, N_HEADS // N_KV_HEADS, HEAD_DIM)
    s = jnp.einsum('btkgd,btnkd->btkgn', qg, kg) * (HEAD_DIM ** -0.5)
    s = jnp.where(valid[:, :, None, None, :], s, -jnp.inf)
    p = jax.nn.softmax(s, axis=-1)
    o = jnp.einsum('btkgn,btnkd->btkgd', p, vg)
    return o.reshape(b, t, ATT_W).astype(q.dtype)

def attend_blocked(q, qi, wi, k, v, ki, top_k):
    b, s = q.shape[:2]
    nb = s // QBLOCK

    def to_blocks(a):
        return jnp.moveaxis(a.reshape((b, nb, QBLOCK) + a.shape[2:]), 1, 0)

    starts = jnp.arange(nb, dtype=jnp.int32) * QBLOCK

    def one(args):
        qb, qib, wib, s0 = args
        pos = s0 + jnp.arange(QBLOCK, dtype=jnp.int32)
        return dsa_attend(qb, qib, wib, k, v, ki, pos, top_k)

    o = lax.map(one, (to_blocks(q), to_blocks(qi), to_blocks(wi), starts))
    return jnp.moveaxis(o, 0, 1).reshape(b, s, ATT_W)

def mixer_layer(x, c, q_pos, top_k, k_past, v_past, ki_past, conv_past,
                norm_g, w_ada, b_ada, w_in, q_norm_g, k_norm_g, idx_k_norm_g,
                conv_w, conv_b, conv_ln_g, conv_ln_b, w_attn_out, w_conv_out, w_out):
    b, t, _ = x.shape
    mod = jax.nn.silu(c) @ w_ada + b_ada
    shift, scale, gate = jnp.split(mod, 3, axis=-1)
    h = rms_norm(x, norm_g) * (1 + scale[:, None]) + shift[:, None]
    zq, zk, zv, zqi, zki, zwi, zga, zglu, zgc, zmerge = split_in(h @ w_in)
    q = rope(rms_norm(zq.reshape(b, t, N_HEADS, HEAD_DIM), q_norm_g), q_pos)
    k = rope(rms_norm(zk.reshape(b, t, N_KV_HEADS, HEAD_DIM), k_norm_g), q_pos)
    v = zv.reshape(b, t, N_KV_HEADS, HEAD_DIM)
    qi = rope(zqi.reshape(b, t, N_IDX_HEADS, IDX_DIM), q_pos)
    ki = rope(rms_norm(zki, idx_k_norm_g)[:, :, None], q_pos)[:, :, 0]
    wi = zwi * (N_IDX_HEADS ** -0.5)
    if k_past is None:
        attn = attend_blocked(q, qi, wi, k, v, ki, top_k)
    else:
        k_all = jnp.concatenate([k_past.astype(k.dtype), k], axis=1)
        v_all = jnp.concatenate([v_past.astype(v.dtype), v], axis=1)
        ki_all = jnp.concatenate([ki_past.astype(ki.dtype), ki], axis=1)
        attn = dsa_attend(q, qi, wi, k_all, v_all, ki_all, q_pos, top_k)
    y_att = (attn * jax.nn.silu(zga)) @ w_attn_out
    za, zb = jnp.split(zglu, 2, axis=-1)
    u = za * jax.nn.sigmoid(zb)
    if conv_past is None:
        conv_past = jnp.zeros((b, CONV_K - 1, CONV_W), u.dtype)
    conv_in = jnp.concatenate([conv_past.astype(u.dtype), u], axis=1)
    new_conv = conv_in[:, -(CONV_K - 1):]
    d = lax.conv_general_dilated(conv_in, conv_w[:, None, :].astype(u.dtype), window_strides=(1,),
                                 padding='VALID', dimension_numbers=('NWC', 'WIO', 'NWC'),
                                 feature_group_count=CONV_W) + conv_b
    d = layer_norm(d, conv_ln_g, conv_ln_b)
    y_conv = (jax.nn.silu(d) * jax.nn.silu(zgc)) @ w_conv_out
    g_att, g_conv = jnp.split(jax.nn.sigmoid(zmerge), 2, axis=-1)
    out = (g_att * y_att + g_conv * y_conv) @ w_out
    x = x + gate[:, None] * out
    return x, k, v, ki, new_conv

def setup_inputs(seed: int = 0) -> dict:
    key = jax.random.key(seed)
    ks = jax.random.split(key, 24)
    n_pages = PAST_LEN // PAGE_SIZE
    n_phys = (DEC_BATCH * n_pages * 5) // 4
    nrm = jax.random.normal
    page_table = jax.random.permutation(ks[8], n_phys)[:DEC_BATCH * n_pages].reshape(DEC_BATCH, n_pages).astype(jnp.int32)
    return {
        'x_prompt': nrm(ks[0], (BATCH, SEQ, D_MODEL), F32),
        'x_sample': nrm(ks[1], (DEC_BATCH, DEC_SEQ, D_MODEL), F32),
        'c_prompt': nrm(ks[2], (BATCH, D_MODEL), F32),
        'c_sample': nrm(ks[3], (DEC_BATCH, D_MODEL), F32),
        'cache_k': nrm(ks[4], (DEPTH, n_phys, PAGE_SIZE, N_KV_HEADS, HEAD_DIM), F32),
        'cache_v': nrm(ks[5], (DEPTH, n_phys, PAGE_SIZE, N_KV_HEADS, HEAD_DIM), F32),
        'cache_kidx': nrm(ks[6], (DEPTH, n_phys, PAGE_SIZE, IDX_DIM), F32),
        'state_conv': 0.5 * nrm(ks[7], (DEPTH, DEC_BATCH, CONV_K - 1, CONV_W), F32),
        'page_table': page_table,
        'norm_g': 1.0 + 0.02 * nrm(ks[9], (DEPTH, D_MODEL), F32),
        'w_ada': 0.5 * D_MODEL ** -0.5 * nrm(ks[10], (DEPTH, D_MODEL, 3 * D_MODEL), F32),
        'b_ada': 0.01 * nrm(ks[11], (DEPTH, 3 * D_MODEL), F32),
        'w_in': D_MODEL ** -0.5 * nrm(ks[12], (DEPTH, D_MODEL, N_IN), F32),
        'q_norm_g': 1.0 + 0.02 * nrm(ks[13], (DEPTH, HEAD_DIM), F32),
        'k_norm_g': 1.0 + 0.02 * nrm(ks[14], (DEPTH, HEAD_DIM), F32),
        'idx_k_norm_g': 1.0 + 0.02 * nrm(ks[15], (DEPTH, IDX_DIM), F32),
        'conv_w': CONV_K ** -0.5 * nrm(ks[16], (DEPTH, CONV_K, CONV_W), F32),
        'conv_b': 0.01 * nrm(ks[17], (DEPTH, CONV_W), F32),
        'conv_ln_g': 1.0 + 0.02 * nrm(ks[18], (DEPTH, CONV_W), F32),
        'conv_ln_b': 0.01 * nrm(ks[19], (DEPTH, CONV_W), F32),
        'w_attn_out': ATT_W ** -0.5 * nrm(ks[20], (DEPTH, ATT_W, D_MODEL), F32),
        'w_conv_out': CONV_W ** -0.5 * nrm(ks[21], (DEPTH, CONV_W, D_MODEL), F32),
        'w_out': D_MODEL ** -0.5 * nrm(ks[22], (DEPTH, D_MODEL, D_MODEL), F32),
    }

def reference(x_prompt, x_sample, c_prompt, c_sample, cache_k, cache_v, cache_kidx, state_conv, page_table,
              norm_g, w_ada, b_ada, w_in, q_norm_g, k_norm_g, idx_k_norm_g,
              conv_w, conv_b, conv_ln_g, conv_ln_b, w_attn_out, w_conv_out, w_out):
    seq = x_prompt.shape[1]
    dec_batch, dec_seq = x_sample.shape[:2]
    n_pages = page_table.shape[1]
    page = cache_k.shape[2]
    past_len = n_pages * page
    pos_p = jnp.arange(seq, dtype=jnp.int32)
    pos_s = past_len + jnp.arange(dec_seq, dtype=jnp.int32)
    topk_p = min(TOPK_MAX, seq // 4)
    topk_s = min(TOPK_MAX, (past_len + dec_seq) // 4)
    xp, xs = x_prompt, x_sample
    kps, vps, kips, cps, kss, vss, kiss, css = [], [], [], [], [], [], [], []
    for l in range(DEPTH):
        lp = (norm_g[l], w_ada[l], b_ada[l], w_in[l], q_norm_g[l], k_norm_g[l], idx_k_norm_g[l],
              conv_w[l], conv_b[l], conv_ln_g[l], conv_ln_b[l], w_attn_out[l], w_conv_out[l], w_out[l])
        xp, kp, vp, kip, cp = mixer_layer(xp, c_prompt, pos_p, topk_p, None, None, None, None, *lp)
        k_past = cache_k[l][page_table].reshape(dec_batch, past_len, N_KV_HEADS, HEAD_DIM)
        v_past = cache_v[l][page_table].reshape(dec_batch, past_len, N_KV_HEADS, HEAD_DIM)
        ki_past = cache_kidx[l][page_table].reshape(dec_batch, past_len, IDX_DIM)
        xs, ks_, vs_, kis_, cs_ = mixer_layer(xs, c_sample, pos_s, topk_s, k_past, v_past, ki_past, state_conv[l], *lp)
        kps.append(kp); vps.append(vp); kips.append(kip); cps.append(cp)
        kss.append(ks_); vss.append(vs_); kiss.append(kis_); css.append(cs_)
    return (xp, xs, jnp.stack(kps), jnp.stack(vps), jnp.stack(kips), jnp.stack(cps),
            jnp.stack(kss), jnp.stack(vss), jnp.stack(kiss), jnp.stack(css))


_drawn_inputs = setup_inputs


def setup_inputs(seed=0):
    import zlib

    import numpy as np

    out = dict(_drawn_inputs(seed))
    spreads = {}
    factors = {'cache_k': 4.664,
     'cache_v': 3.641,
     'cache_kidx': 3.973,
     'norm_g': 2.694,
     'b_ada': 3.951,
     'q_norm_g': 8.0,
     'k_norm_g': 2.905,
     'idx_k_norm_g': 2.765,
     'conv_b': 8.0,
     'conv_ln_g': 8.0,
     'conv_ln_b': 8.0}
    for name, (base, spread) in spreads.items():
        noise = np.random.default_rng([zlib.crc32(name.encode()), seed]).standard_normal(out[name].shape)
        drawn = base * np.exp(spread * noise) if base else spread * noise
        out[name] = __import__('jax').numpy.asarray(drawn.astype(out[name].dtype))
    for name, factor in factors.items():
        out[name] = (out[name] * factor).astype(out[name].dtype)
    return out
```

```python
from contextlib import ExitStack

import concourse.bass as bass
from concourse import mybir

F32 = mybir.dt.float32
F32R = mybir.dt.float32r
I32 = mybir.dt.int32
ACT = mybir.ActivationFunctionType
ALU = mybir.AluOpType
AX_X = mybir.AxisListType.X
ds = bass.ds

P = 128
DEPTH, DM, SEQ, SEQS, STEPS = 2, 2048, 512, 8, 4
NS = SEQS * STEPS
TOK = SEQ + NS
HALF = TOK // 2
KT = DM // P
PAST, PAGE = 2048, 128
PAGES = PAST // PAGE
NKEY = PAST + STEPS
HEADS, HD, KVH, IH, ID = 8, 128, 2, 16, 64
GROUP = HEADS // KVH
ATT, KVW, CW_, TAPS = HEADS * HD, KVH * HD, DM // 2, 31
HIST = TAPS - 1
TOPK_P = min(256, SEQ // 4)
TOPK_S = min(256, NKEY // 4)
EPS = 1e-6
NEG = -3.0e38
BIG = 1.0e30
QT = SEQ // P
CT_ = CW_ // P

C_Q = 0
C_K = C_Q + ATT
C_V = C_K + KVW
C_QI = C_V + KVW
C_KI = C_QI + IH * ID
C_WI = C_KI + ID
C_GA = C_WI + IH
C_GLU = C_GA + ATT
C_GC = C_GLU + 2 * CW_
C_MG = C_GC + CW_

G_ADA, G_IN, G_MG, G_OUT = 0, 24, 67, 75
G_Q, G_K, G_V, G_QI, G_KI = 24, 28, 29, 30, 34
G_GLU, G_MERGE, G_GA, G_GC = 35, 43, 59, 63
N_GROUPS = 83

R_NORM, R_BADA, R_QG, R_KG, R_IG, R_CB, R_LG, R_LB, N_PAR = 0, 16, 64, 65, 66, 67, 75, 83, 91

T_ID, T_ONE, T_ONE64, T_SWQ, T_SWI = 0, 128, 256, 384, 512
T_CQ, T_SQ, T_CI, T_SI = 640, 640 + TOK, 640 + 2 * TOK, 640 + 3 * TOK
T_TRI = 640 + 4 * TOK
T_TRIB = T_TRI + 128
T_UMS = T_TRIB + 128
T_COMB = T_UMS + STEPS
T_EXP = T_COMB + 9
T_MASK = T_EXP + 64
N_TAB = T_MASK + SEQS * NS


def tables():
    import numpy as np

    t = np.zeros((P, N_TAB), np.float32)
    t[:, T_ID:T_ID + P] = np.eye(P)
    t[:, T_ONE:T_ONE + P] = 1.0
    for a in range(2):
        t[64 * a:64 * a + 64, T_ONE64 + 64 * a:T_ONE64 + 64 * a + 64] = 1.0
    pos = np.concatenate([np.arange(SEQ), np.tile(PAST + np.arange(STEPS), SEQS)]).astype(np.float32)
    for dim, swap, cos, sin in ((HD, T_SWQ, T_CQ, T_SQ), (ID, T_SWI, T_CI, T_SI)):
        half = dim // 8
        inv = np.float32(500000.0) ** (-(np.arange(half, dtype=np.float32) / np.float32(half)))
        ang = (pos[:, None] * inv[None, :].astype(np.float32)).astype(np.float32)
        c, s = np.cos(ang).T, np.sin(ang).T
        t[:, cos:cos + TOK] = 1.0
        for r in range(0, P, dim):
            t[r:r + half, cos:cos + TOK] = c
            t[r + half:r + 2 * half, cos:cos + TOK] = c
            t[r:r + half, sin:sin + TOK] = -s
            t[r + half:r + 2 * half, sin:sin + TOK] = s
            for d in range(half):
                t[r + d + half, swap + r + d] = 1.0
                t[r + d, swap + r + d + half] = 1.0
    q, k = np.arange(P)[:, None], np.arange(P)[None, :]
    t[:, T_TRI:T_TRI + P] = np.where(k <= q, 3.4e38, NEG)
    t[:, T_TRIB:T_TRIB + P] = np.where(k <= q, 0.0, -BIG)
    r = np.arange(NS)
    t[:NS, T_UMS:T_UMS + STEPS] = np.where(np.arange(STEPS)[None, :] <= (r % STEPS)[:, None], 3.4e38, NEG)
    for a in range(2):
        t[9 * a:9 * a + 9, T_COMB:T_COMB + 9] = np.eye(9)
    for h in range(IH):
        for s in range(STEPS):
            t[h, T_EXP + 32 * (h % 2) + STEPS * (h // 2) + s] = 1.0
    for row in range(64):
        for b in range(SEQS):
            t[row, T_MASK + b * NS + STEPS * b + row % STEPS] = 1.0
    return t


def trunk_kernel(nc, x_prompt, x_sample, c_prompt, c_sample, cache_k, cache_v, cache_kidx, state_conv, page_table,
                 norm_g, w_ada, b_ada, w_in, q_norm_g, k_norm_g, idx_k_norm_g, conv_w, conv_b, conv_ln_g, conv_ln_b,
                 w_attn_out, w_conv_out, w_out, table,
                 y_prompt, y_sample, k_prompt, v_prompt, ki_prompt, cv_prompt, k_sample, v_sample, ki_sample, cv_sample):
    n_phys = cache_k.shape[1]
    with ExitStack() as ctx:
        def sb(name, shape, dt=F32):
            return ctx.enter_context(nc.sbuf_tensor(name, shape, dt))

        x_spill = nc.dram_tensor("x_spill", [P, KT, TOK], F32).ap()
        q_spill = nc.dram_tensor("q_spill", [P, HEADS, TOK], F32).ap()
        gate_spill = nc.dram_tensor("gate_spill", [P, 2 * KT, TOK], F32).ap()
        ga_spill = nc.dram_tensor("ga_spill", [P, HEADS, TOK], F32).ap()
        bias_spill = nc.dram_tensor("bias_spill", [NS, NKEY], F32).ap()

        with ExitStack() as area:
            x_rows = area.enter_context(nc.sbuf_tensor("x_rows", [P, 5, DM], F32))
            c_rows = area.enter_context(nc.sbuf_tensor("c_rows", [9, DM], F32))
        with ExitStack() as area:
            q_att = area.enter_context(nc.sbuf_tensor("q_att", [P, HEADS, TOK], F32))
            k_pages = area.enter_context(nc.sbuf_tensor("k_pages", [P, PAGES, KVW], F32))
            v_pages = area.enter_context(nc.sbuf_tensor("v_pages", [P, PAGES, KVW], F32))
            k_turned = area.enter_context(nc.sbuf_tensor("k_turned", [P, KVH, NKEY], F32))
            p_turned = area.enter_context(nc.sbuf_tensor("p_turned", [P, PAGES + 1, NS], F32))
            q_one = area.enter_context(nc.sbuf_tensor("q_one", [P, KVH, NS], F32))
        act_hi = sb("act_hi", [P, KT, TOK], F32R)
        act_lo = sb("act_lo", [P, KT, TOK], F32R)

        tab = sb("tab", [P, N_TAB])
        raw = sb("raw", [P, 4, 4, 256])
        w_hi_t = sb("w_hi_t", [P, 2, 4, 256], F32R)
        w_lo_t = sb("w_lo_t", [P, 2, 4, 256], F32R)
        x_t = sb("x_t", [P, KT * TOK])
        d_t = sb("d_t", [P, 8, TOK])
        stg = sb("stg", [P, 8 * TOK])
        k_new = sb("k_new", [P, KVH, TOK])
        ki_new = sb("ki_new", [P, TOK])
        wi_new = sb("wi_new", [IH, TOK])
        v_tok = sb("v_tok", [P, 5, KVW])
        k_tok = sb("k_tok", [P, 5, KVW])
        ki_tok = sb("ki_tok", [P, 5, ID])
        wi_tok = sb("wi_tok", [P, QT, IH])
        wi_mix = sb("wi_mix", [64, SEQS, NS])
        c_split = sb("c_split", [P, KT, 18], F32R)
        mod = sb("mod", [P, 48, 9])
        par_rows = sb("par_rows", [N_PAR, P])
        par = sb("par", [P, N_PAR])
        cw = sb("cw", [P, CT_, TAPS])
        pages = sb("pages", [1, SEQS * PAGES], I32)
        top8 = sb("top8", [P, 8])
        stat = sb("stat", [P, 16])
        eps = sb("eps", [P, 1])

        acc = ctx.enter_context(nc.psum_tensor("acc", [P, 4, 512], F32))
        aux = ctx.enter_context(nc.psum_tensor("aux", [P, 4, 512], F32))

        ident = tab[:, T_ID:T_ID + P]
        ones = tab[:, T_ONE:T_ONE + P]

        def pair(ap):
            return ap.rearrange("p (h n) -> p h n", h=2)

        def tabv(c):
            return pair(tab[:, c:c + TOK])

        def slot(i):
            return stg[:, i * TOK:(i + 1) * TOK]

        def samp(ap):
            return ap.rearrange("p (b t) -> p b t", t=STEPS)

        x_v = x_t[:, :].rearrange("p (k n) -> p k n", k=KT)
        X8 = 8 * TOK

        def xtile(k):
            return x_t[:, ds(k * TOK, TOK)] if not isinstance(k, int) else x_t[:, k * TOK:(k + 1) * TOK]

        NPR = P * (1 + 2 + 3 + 4)
        qoff = [0, P, 3 * P, 6 * P]
        work_p = x_t[:, 0:NPR]
        work_s = x_t[0:NS, NPR:NPR + NKEY]
        attn_o = x_v[:, 0:8, :]
        bias_p = x_t[:, X8:X8 + NPR]
        bias_s = x_t[0:NS, X8 + NPR:X8 + NPR + NKEY]
        state_rows = x_t[0:120, NPR + NKEY:NPR + NKEY + 512].rearrange("p (s h n) -> p s h n", s=2, h=2)
        tail2 = X8 + NPR + NKEY
        qi_all = x_t[:, tail2:tail2 + SEQS * 64].rearrange("p (b n) -> p b n", b=SEQS)
        u_tok = x_t[0:NS, tail2:tail2 + 512].rearrange("p (s h n) -> p s h n", s=2, h=2)
        p_tail = x_t[0:NS, tail2 + 512:tail2 + 512 + NS]
        conv_rows = stg[0:TAPS, 6 * TOK:6 * TOK + CW_]
        UB = SEQ + HIST + SEQS * (HIST + STEPS)
        u_pad = [stg[:, 4 * TOK + s * UB:4 * TOK + (s + 1) * UB] for s in range(2)]
        relu_p = stg[:, 0:2048].rearrange("p (s h n) -> p s h n", s=2, h=2)
        kx_pages = stg[:, 0:2048].rearrange("p (s g n) -> p s g n", s=2, g=PAGES)
        kx_turned = stg[:, 2048:2560].rearrange("p (s n) -> p s n", s=2)
        relu_s = stg[0:64, 3072:4096].rearrange("p (s n) -> p s n", s=2)
        relu_tail = stg[0:64, 4096:4096 + NS]
        probs_p = stg[:, 0:4096].rearrange("p (s h n) -> p s h n", s=2, h=4)
        pt_p = k_turned[:, 0, 0:1024].rearrange("p (s n) -> p s n", s=2)
        probs_s = stg[0:NS, 0:NKEY]
        bias_rep = stg[0:NS, NKEY:2 * NKEY]

        def accv(m):
            return acc[:, 2 * m:2 * m + 2, 0:HALF]

        names = """passed w_landed0 w_landed1 w_landed2 w_landed3 w_hi w_lo w_used acc0_ready acc0_free acc1_free
            params_in params_turned params_done state_copied row_ready mod_turned mod_done
            sq_ready xsum ssq_x rstd_x h_ready h_hi h_lo
            aux_ready swap_used std_ready rope_done tok_turned tok_done tok_stored q_spilled
            dots_ready relu_done score_done kx_landed0 kx_landed1 kx_turned_ps kx_copied sdots_ready srelu_done mixed score_s_done diag_done
            state_in0 state_in1 state_turned state_used glu_staged u_done u_turned u_copied u_stored0 u_stored1
            mean_in mean_ps mean_done cent_done csq_done cvar_in var_ps cstd_done ln_done silu_done
            act_stored0 act_stored1 gc_done
            bias_done bias_stored q_back logits_p probs_raw ppeak_done exp_p p_ready ptr_p ptc_p pv_p ao_p
            k_landed v_landed k_turn_a k_turn_b k_cp_a k_cp_b q_one_done logits_s brep_in sraw_done exp_s ps_ready pts_ps pts_done pv_s ao_s
            ga_in0 ga_in1 ga_in2 ga_in3 ag_ready split_hi split_lo gates_in0 gates_in1 gates_used merged_hi merged_lo x_old_in0 x_old_in1 x_new_done x_stored
            dve act_own arrived""".split()
        sems = {n: ctx.enter_context(nc.semaphore(n)) for n in names}
        layer_sems = range(sems["passed"].num, sems["arrived"].num + 1)
        assert len(layer_sems) == len(names)
        S = type("Sems", (), sems)
        w_landed = [S.w_landed0, S.w_landed1, S.w_landed2, S.w_landed3]
        acc_free = [S.acc0_free, S.acc1_free]
        kx_landed, state_in, u_stored = [S.kx_landed0, S.kx_landed1], [S.state_in0, S.state_in1], [S.u_stored0, S.u_stored1]
        act_stored, gates_in, x_old_in = [S.act_stored0, S.act_stored1], [S.gates_in0, S.gates_in1], [S.x_old_in0, S.x_old_in1]
        ga_in = [S.ga_in0, S.ga_in1, S.ga_in2, S.ga_in3]
        layer_go = ctx.enter_context(nc.semaphore("layer_go"))
        tables_in = ctx.enter_context(nc.semaphore("tables_in"))
        rows_in = ctx.enter_context(nc.semaphore("rows_in"))
        pro_turned = ctx.enter_context(nc.semaphore("pro_turned"))
        pro_copied = ctx.enter_context(nc.semaphore("pro_copied"))
        pro_c = ctx.enter_context(nc.semaphore("pro_c"))
        pro_stored = ctx.enter_context(nc.semaphore("pro_stored"))
        eps_set = ctx.enter_context(nc.semaphore("eps_set"))
        y_turned = ctx.enter_context(nc.semaphore("y_turned"))
        y_copied = ctx.enter_context(nc.semaphore("y_copied"))
        y_stored = ctx.enter_context(nc.semaphore("y_stored"))
        block = ctx.enter_context(nc.Block())

        def hold(e, s, value):
            e.wait_ge(s, value)
            if not isinstance(value, int):
                e.sem_inc(S.passed, 1)

        class Steps:

            def __init__(self, e, s):
                self.e, self.s, self.n = e, s, 0

            def then(self, ins):
                ins.then_inc(self.s, 1)
                self.n += 1

            def wait(self, back=0):
                self.e.wait_ge(self.s, self.n - back)

            def close(self):
                self.wait()
                self.e.sem_clear(self.s)
                self.n = 0

        def end_of_layer(e, turn, clears=False):
            e.drain().then_inc(S.arrived, 1)
            if clears:
                e.wait_ge(S.arrived, 5)
                e.sem_clear(layer_sems)
                e.sem_inc(layer_go, 1)
            else:
                e.wait_ge(layer_go, turn)
                e.nop() if isinstance(turn, int) else e.sem_inc(S.passed, 1)

        TT = [(0, P), (P, P), (2 * P, P), (3 * P, P), (SEQ, NS)]

        @block.sync
        def _(sp):
            sp.dma_start(tab[:, :], table).then_inc(tables_in, 16)
            sp.dma_start(pages[:, :], page_table.rearrange("(a b) n -> a (b n)", a=1)).then_inc(tables_in, 16)
            sp.dma_start(c_rows[0:1, :], c_prompt).then_inc(rows_in, 16)
            sp.dma_start(c_rows[1:9, :], c_sample).then_inc(rows_in, 16)
            sp.dma_start(x_rows[:, 0:4, :], x_prompt.rearrange("a (t p) n -> p (a t) n", p=P)).then_inc(rows_in, 16)
            sp.dma_start(x_rows[0:NS, 4, :], x_sample.rearrange("b t n -> (b t) n")).then_inc(rows_in, 16)
            sp.wait_ge(pro_copied, 2 * KT)
            sp.dma_start(x_spill, x_v).then_inc(pro_stored, 16)
            sp.wait_ge(pro_stored, 16)
            sp.wait_ge(tables_in, 32)
            end_of_layer(sp, 1, clears=True)

            def load(i, g, pieces):
                hold(sp, S.w_lo, 4 * g + i + 1)
                for dst, src, inc in pieces:
                    sp.dma_start(dst, src.rearrange("a (t p) n -> p (a t) n", p=P)).then_inc(w_landed[i], inc)

            with sp.Fori(0, DEPTH) as l:
                sp.sem_inc(S.w_lo, 4)
                one = ds(l, 1)
                for r0, n, src in ((R_NORM, 16, norm_g), (R_BADA, 48, b_ada), (R_QG, 1, q_norm_g), (R_KG, 1, k_norm_g),
                                   (R_CB, 8, conv_b), (R_LG, 8, conv_ln_g), (R_LB, 8, conv_ln_b)):
                    sp.dma_start(par_rows[r0:r0 + n, :], src[one, :].rearrange("a (r p) -> (a r) p", p=P)).then_inc(S.params_in, 16)
                for a in range(2):
                    sp.dma_start(par_rows[R_IG:R_IG + 1, 64 * a:64 * a + 64], idx_k_norm_g[one, :]).then_inc(S.params_in, 16)
                sp.dma_start(conv_rows, conv_w[one].rearrange("a k c -> (a k) c")).then_inc(S.params_in, 16)
                sp.dma_start(cv_sample[one, :, 0:HIST - STEPS, :].rearrange("a b k c -> (a b) k c"),
                             state_conv[one, :, STEPS:HIST, :].rearrange("a b k c -> (a b) k c")).then_inc(S.state_copied, 16)
                with sp.Fori(0, 24) as c:
                    for i in range(4):
                        load(i, c, [(raw[:, i], w_ada[one, 512 * i:512 * i + 512, ds(c * 256, 256)], 48)])

                def load_in(g0, n, col):
                    with sp.Fori(0, n) as c:
                        for i in range(4):
                            load(i, g0 + c, [(raw[:, i], w_in[one, 512 * i:512 * i + 512, ds(c * 256 + col, 256)], 48)])

                load_in(G_Q, 10, C_Q)
                for i in range(4):
                    rows = slice(512 * i, 512 * i + 512)
                    load(i, G_KI, [(raw[:, i, :, 0:64], w_in[one, rows, C_KI:C_KI + ID], 16),
                                   (raw[:, i, :, 64:128], w_in[one, rows, C_KI:C_KI + ID], 16),
                                   (raw[:, i, :, 128:256], w_in[one, rows, C_WI:C_WI + P], 16)])

                def load_glu(c):
                    for i in range(4):
                        rows = slice(512 * i, 512 * i + 512)
                        load(i, G_GLU + c, [(raw[:, i, :, 0:128], w_in[one, rows, ds(c * P + C_GLU, P)], 16),
                                            (raw[:, i, :, 128:256], w_in[one, rows, ds(c * P + (C_GLU + CW_), P)], 32)])

                load_glu(0)
                sp.wait_ge(S.rope_done, 2 + 21)
                sp.dma_start(q_spill, x_v[:, 0:8, :]).then_inc(S.q_spilled, 16)
                sp.wait_ge(S.tok_done, 1)
                for dst, dsts, src in ((k_prompt, k_sample, k_tok), (v_prompt, v_sample, v_tok)):
                    sp.dma_start(dst[one].rearrange("a b (t p) h d -> p (a b t) (h d)", p=P), src[:, 0:4, :]).then_inc(S.tok_stored, 16)
                    sp.dma_start(dsts[one].rearrange("a b t h d -> (a b t) (h d)"), src[0:NS, 4, :]).then_inc(S.tok_stored, 16)
                sp.dma_start(ki_prompt[one].rearrange("a b (t p) d -> p (a b t) d", p=P), ki_tok[:, 0:4, :]).then_inc(S.tok_stored, 16)
                sp.dma_start(ki_sample[one].rearrange("a b t d -> (a b t) d"), ki_tok[0:NS, 4, :]).then_inc(S.tok_stored, 16)
                sp.wait_ge(S.score_done, 32)
                for b in range(SEQS):
                    if b >= 2:
                        sp.wait_ge(S.kx_turned_ps, 4 * (b - 1))
                    with sp.Fori(0, PAGES) as g:
                        page = sp.value_load(pages[0:1, ds(g + b * PAGES, 1)], min_val=0, max_val=n_phys - 1)
                        sp.dma_start(kx_pages[:, b % 2, ds(g, 1), :],
                                     cache_kidx[one, ds(page, 1)].rearrange("a g p d -> p (a g) d")).then_inc(kx_landed[b % 2], 16)
                def load_state(c, s):
                    hold(sp, S.state_used, c + 1)
                    sp.dma_start(state_rows[:, s], state_conv[one].rearrange("a b k c -> (a b k) c")[:, ds(c * P, P)].rearrange(
                        "(h r) c -> r h c", h=2)).then_inc(state_in[s], 16)

                sp.wait_ge(S.q_spilled, 16)
                with sp.Fori(0, 3) as cc:
                    for s in range(2):
                        load_state(cc * 2 + s, s)
                        load_glu(cc * 2 + (s + 1))
                load_state(6, 0)
                load_glu(7)
                load_state(7, 1)
                load_in(G_MERGE, 16, C_MG)
                load_in(G_GA, 4, C_GA)
                load_in(G_GC, 4, C_GC)

                def load_branches(c):
                    for i in range(4):
                        w = w_attn_out if i < 2 else w_conv_out
                        load(i, G_MG + c, [(raw[:, i], w[one, 512 * (i % 2):512 * (i % 2) + 512, ds(c * 256, 256)], 48)])

                load_branches(0)
                sp.wait_ge(S.w_used, 4 * G_MG + 2)
                sp.dma_start(q_att[:, :, :], q_spill).then_inc(S.q_back, 16)
                sp.wait_ge(S.bias_done, 1)
                sp.dma_start(bias_spill, bias_s).then_inc(S.bias_stored, 16)
                with sp.Fori(0, SEQS) as b:
                    hold(sp, S.k_turn_a, 4 * b + 4)
                    hold(sp, S.k_turn_b, 4 * b + 4)
                    with sp.Fori(0, PAGES) as g:
                        page = sp.value_load(pages[0:1, ds(b * PAGES + g, 1)], min_val=0, max_val=n_phys - 1)
                        sp.dma_start(k_pages[:, ds(g, 1), :], cache_k[one, ds(page, 1)].rearrange(
                            "a g p h d -> p (a g) (h d)")).then_inc(S.k_landed, 16)
                    sp.wait_ge(S.bias_stored, 16)
                    sp.wait_ge(S.ao_p, 8)
                    hold(sp, S.sraw_done, b + 1)
                    for r in range(HEADS):
                        sp.dma_start(bias_rep[STEPS * r:STEPS * r + STEPS, :], bias_spill[ds(b * STEPS, STEPS), :]).then_inc(S.brep_in, 16)
                    hold(sp, S.pv_s, b + 1)
                    with sp.Fori(0, PAGES) as g:
                        page = sp.value_load(pages[0:1, ds(b * PAGES + g, 1)], min_val=0, max_val=n_phys - 1)
                        sp.dma_start(v_pages[:, ds(g, 1), :], cache_v[one, ds(page, 1)].rearrange(
                            "a g p h d -> p (a g) (h d)")).then_inc(S.v_landed, 16)
                sp.wait_ge(S.ao_s, 8)
                for h in range(HEADS):
                    if h >= 4:
                        sp.wait_ge(S.ag_ready, h - 3)
                    sp.dma_start(slot(h % 4), ga_spill[:, h, :]).then_inc(ga_in[h % 4], 16)
                def load_gates(c, s):
                    sp.wait_ge(S.split_lo, 16)
                    hold(sp, S.gates_used, c + 1)
                    for a in range(2):
                        sp.dma_start(stg[:, (4 * s + 2 * a) * TOK:(4 * s + 2 * a + 2) * TOK].rearrange("p (k n) -> p k n", k=2),
                                     gate_spill[:, ds(c * 2 + a * KT, 2), :]).then_inc(gates_in[s], 16)

                with sp.Fori(0, 3) as cc:
                    for s in range(2):
                        load_gates(cc * 2 + s, s)
                        load_branches(cc * 2 + (s + 1))
                load_gates(6, 0)
                load_branches(7)
                load_gates(7, 1)
                with sp.Fori(0, 4) as cc:
                    for s in range(2):
                        c = cc * 2 + s
                        for i in range(4):
                            load(i, G_OUT + c, [(raw[:, i], w_out[one, 512 * i:512 * i + 512, ds(c * 256, 256)], 48)])
                        sp.wait_ge(S.gates_used, 2 + 8)
                        hold(sp, S.x_new_done, c * 2 + 2)
                        sp.dma_start(stg[:, 2 * s * TOK:(2 * s + 2) * TOK].rearrange("p (k n) -> p k n", k=2),
                                     x_spill[:, ds(c * 2, 2), :]).then_inc(x_old_in[s], 16)
                sp.wait_ge(S.x_new_done, 4 + KT)
                sp.dma_start(x_spill, x_v).then_inc(S.x_stored, 16)
                sp.wait_ge(S.x_stored, 16)
                sp.wait_ge(S.tok_stored, 16 * 6)
                sp.wait_ge(S.state_copied, 16)
                end_of_layer(sp, None, clears=True)
            for t, (t0, n) in enumerate(TT):
                sp.wait_ge(y_copied, 4 * (t + 1))
                dst = y_prompt[0, t0:t0 + n, :] if t < 4 else y_sample.rearrange("b t n -> (b t) n")
                sp.dma_start(dst, x_rows[0:n, t, :]).then_inc(y_stored, 16)
            sp.wait_ge(y_stored, 16 * 5)

        @block.gpsimd
        def _(pool):
            end_of_layer(pool, 1)

            def lo(i, g):
                hold(pool, S.w_hi, 4 * g + i + 1)
                pool.tensor_tensor(w_lo_t[:, i % 2], raw[:, i], w_hi_t[:, i % 2].bitcast(F32), ALU.subtract).then_inc(S.w_lo, 1)

            def groups(g0, n):
                with pool.Fori(0, n) as c:
                    lo(2, g0 + c)
                    lo(3, g0 + c)
                    lo(0, g0 + c + 1)
                    lo(1, g0 + c + 1)

            with pool.Fori(0, DEPTH) as l:
                pool.sem_inc(S.h_lo, 2)
                lo(0, 0)
                lo(1, 0)
                groups(0, 24)
                with pool.Fori(0, KT // 2) as kk:
                    for s in range(2):
                        kt = kk * 2 + s
                        hold(pool, S.h_hi, kt + 1)
                        pool.tensor_tensor(act_lo[:, ds(kt, 1), :].rearrange("p a n -> p (a n)"), slot(4 + s),
                                           act_hi[:, ds(kt, 1), :].rearrange("p a n -> p (a n)").bitcast(F32), ALU.subtract).then_inc(S.h_lo, 1)
                groups(G_IN, 43)
                for n in range(16):
                    pool.wait_ge(S.split_hi, n + 1)
                    dst, src = (act_hi, d_t[:, n, :]) if n < 8 else (act_lo, slot(4 + n % 4))
                    pool.tensor_tensor(dst[:, 8 + n % 8, :], src, dst[:, n % 8, :].bitcast(F32), ALU.subtract).then_inc(S.split_lo, 1)
                groups(G_MG, 8)
                for k in range(KT):
                    pool.wait_ge(S.merged_hi, k + 1)
                    pool.tensor_tensor(act_lo[:, k, :], xtile(k), act_hi[:, k, :].bitcast(F32), ALU.subtract).then_inc(S.merged_lo, 1)
                groups(G_OUT, 7)
                lo(2, N_GROUPS - 1)
                lo(3, N_GROUPS - 1)
                end_of_layer(pool, l + 2)

        @block.scalar
        def _(act):
            act.wait_ge(eps_set, 1)
            for k in range(KT):
                act.wait_ge(pro_turned, k + 1)
                act.activation(x_v[:, k, 0:SEQ], acc[:, 2 * (k % 2), :], ACT.Copy).then_inc(pro_copied, 1)
                act.activation(x_v[:, k, SEQ:TOK], acc[:, 2 * (k % 2) + 1, 0:NS], ACT.Copy).then_inc(pro_copied, 1)
            act.wait_ge(pro_turned, KT + 1)
            act.activation(slot(0)[:, 0:144], aux[:, 0, 0:144], ACT.Silu).then_inc(pro_c, 1)
            act.wait_ge(pro_c, 1)
            act.activation(c_split[:, :, 0:9], slot(0)[:, 0:144].rearrange("p (k n) -> p k n", n=9), ACT.Copy).then_inc(pro_c, 1)
            end_of_layer(act, 1)

            def hi(i, g):
                hold(act, w_landed[i], 48 * g + 48)
                hold(act, S.w_used, 4 * g + i + 1)
                act.activation(w_hi_t[:, i % 2], raw[:, i], ACT.Copy).then_inc(S.w_hi, 1)

            own = Steps(act, S.act_own)

            with act.Fori(0, DEPTH) as l:
                hi(0, 0)
                hi(1, 0)
                with act.Fori(0, KT // 2) as kk:
                    for s in range(2):
                        kt = kk * 2 + s
                        hold(act, S.xsum, kt + 1)
                        act.activation(slot(s), xtile(kt), ACT.Square).then_inc(S.sq_ready, 1)
                with act.Fori(0, 12) as cc:
                    for s in range(2):
                        g = cc * 2 + s
                        hi(2, g)
                        hi(3, g)
                        hi(0, g + 1)
                        hold(act, S.w_used, 4 * g + 4 + 2)
                        hold(act, S.mod_turned, g + 1)
                        act.activation(slot(7)[0:18, 256 * s:256 * s + 256], acc[0:18, 2 * s, 0:256], ACT.Copy).then_inc(S.row_ready, 1)
                        hi(1, g + 1)
                act.wait_ge(S.ssq_x, 1)
                act.activation(pair(slot(3)), aux[:, 0:2, 0:HALF], ACT.Sqrt, scale=1.0 / DM, bias=eps[:, :]).then_inc(S.rstd_x, 1)
                with act.Fori(0, KT // 2) as kk:
                    for s in range(2):
                        kt = kk * 2 + s
                        hold(act, S.h_ready, kt + 1)
                        act.activation(act_hi[:, ds(kt, 1), :].rearrange("p a n -> p (a n)"), slot(4 + s), ACT.Copy).then_inc(S.h_hi, 1)

                def ready(m, g, a0):
                    if m == 0:
                        hold(act, S.acc0_ready, a0 + 1)
                    else:
                        hold(act, S.w_used, 4 * g + 6)

                def project1(g, t, gains, squares, aux_n, std_n, n_dim):
                    hi(2, g)
                    hi(3, g)
                    hi(0, g + 1)
                    for m in range(2):
                        if m == 1:
                            hi(1, g + 1)
                        ready(m, g, g - G_IN)
                        if gains[m] == "wi":
                            act.activation(pair(wi_new[:, :]), acc[0:IH, 2:4, 0:HALF], ACT.Copy,
                                           scale=IH ** -0.5 * ID ** -0.5).then_inc(acc_free[m], 1)
                            continue
                        hold(act, S.rope_done, t + m + 1)
                        gain = gains[m]
                        one_op = act.activation(pair(slot(m)), accv(m), ACT.Copy, scale=1.0 if gain is None else par[:, gain:gain + 1])
                        if squares:
                            one_op = act.activation(pair(slot(2 + m)), accv(m), ACT.Square)
                        one_op.then_inc(acc_free[m], 1)
                    if squares:
                        for m in range(squares):
                            hold(act, S.aux_ready, aux_n + m + 1)
                            act.activation(pair(slot(4 + m)), aux[:, 0:2, 0:HALF], ACT.Sqrt, scale=1.0 / n_dim,
                                           bias=eps[:, :]).then_inc(S.std_ready, 1)

                with act.Fori(0, 4) as c:
                    project1(G_Q + c, c * 2, (R_QG, R_QG), 2, c * 2, c * 2, HD)
                project1(G_K, 8, (R_KG, R_KG), 2, 8, 8, HD)
                project1(G_V, 10, (None, None), 0, 10, 10, HD)
                with act.Fori(0, 4) as c:
                    project1(G_QI + c, c * 2 + 12, (None, None), 0, 0, 0, ID)
                project1(G_KI, 20, (R_IG, "wi"), 1, 20, 10, ID)

                for u in range(4 * 8):
                    n = P * (u // 8 + 1)
                    act.wait_ge(S.dots_ready, u + 1)
                    if u >= 2:
                        act.wait_ge(S.score_done, u - 1)
                    act.activation(relu_p[:, u % 2, :, 0:n], aux[:, 2 * (u % 2):2 * (u % 2) + 2, 0:n], ACT.Relu).then_inc(S.relu_done, 1)
                for f in range(4 * SEQS):
                    act.wait_ge(S.kx_turned_ps, f + 1)
                    if f >= 2:
                        act.wait_ge(S.sdots_ready, f - 1)
                    act.activation(kx_turned[:, f % 2, :], aux[:, 0, 0:256], ACT.Copy).then_inc(S.kx_copied, 1)

                for s in range(2):
                    act.sem_inc(u_stored[s], 32)
                    act.sem_inc(act_stored[s], 16)
                with act.Fori(0, 4) as cc:
                    for s in range(2):
                        c = cc * 2 + s
                        g = G_GLU + c
                        hi(2, g)
                        hi(3, g)
                        hi(0, g + 1)
                        ready(0, g, g - G_IN)
                        hold(act, S.u_done, c + 1)
                        act.activation(pair(slot(s)), accv(0), ACT.Copy).then_inc(acc_free[0], 1)
                        hi(1, g + 1)
                        ready(1, g, None)
                        act.activation(pair(slot(2 + s)), accv(1), ACT.Sigmoid).then_inc(acc_free[1], 1)
                        hold(act, S.u_turned, c + 1)
                        hold(act, u_stored[s], cc * 32 + 32)
                        act.activation(u_tok[:, s], aux[0:NS, 1, 0:256].rearrange("p (h n) -> p h n", h=2), ACT.Copy).then_inc(S.u_copied, 1)
                        hold(act, S.u_copied, c + 1)
                        act.dma_start(cv_prompt[ds(l, 1), :, :, ds(c * P, P)].rearrange("a b k c -> (a b k) c"),
                                      u_tok[0:HIST, s, 0, :]).then_inc(u_stored[s], 16)
                        act.dma_start(cv_sample[ds(l, 1), :, HIST - STEPS:HIST, ds(c * P, P)].rearrange("a b k c -> (a b) k c"),
                                      u_tok[:, s, 1, :]).then_inc(u_stored[s], 16)
                act.wait_ge(S.u_done, 2 + 8)

                def gates(g0, n, n0, func, dst, tile0):
                    with act.Fori(0, n) as c:
                        g = g0 + c
                        hi(2, g)
                        hi(3, g)
                        hi(0, g + 1)
                        for m in range(2):
                            if m == 1:
                                hi(1, g + 1)
                            ready(m, g, g - G_IN)
                            hold(act, act_stored[m], c * 16 + (n0 // 2 + 1) * 16)
                            act.activation(pair(slot(m)), accv(m), func).then_inc(acc_free[m], 1)
                            hold(act, acc_free[m], g - G_IN + 2)
                            act.dma_start(dst[:, ds(c * 2 + (tile0 + m), 1), :].rearrange("p a n -> p (a n)"), slot(m)).then_inc(act_stored[m], 16)

                gates(G_MERGE, 4, 0, ACT.Sigmoid, gate_spill, 0)
                act.wait_ge(S.mean_ps, 1)
                act.activation(pair(slot(2)), aux[:, 0:2, 0:HALF], ACT.Copy, scale=1.0 / CW_).then_inc(S.mean_done, 1)
                for j in range(CT_):
                    act.wait_ge(S.cent_done, j + 1)
                    if j >= 2:
                        act.wait_ge(S.cvar_in, j - 1)
                    act.activation(slot(4 + j % 2), d_t[:, j, :], ACT.Square).then_inc(S.csq_done, 1)
                gates(G_MERGE + 4, 4, 8, ACT.Sigmoid, gate_spill, 8)
                act.wait_ge(S.var_ps, 1)
                act.activation(pair(slot(3)), aux[:, 2:4, 0:HALF], ACT.Sqrt, scale=1.0 / CW_, bias=eps[:, :]).then_inc(S.cstd_done, 1)
                for j in range(CT_):
                    act.wait_ge(S.ln_done, j + 1)
                    act.activation(d_t[:, j, :], d_t[:, j, :], ACT.Silu, scale=par[:, R_LG + j:R_LG + j + 1],
                                   bias=par[:, R_LB + j:R_LB + j + 1]).then_inc(S.silu_done, 1)
                gates(G_MERGE + 8, 8, 16, ACT.Sigmoid, gate_spill, 16)
                gates(G_GA, 4, 32, ACT.Silu, ga_spill, 0)
                for m in range(2):
                    act.wait_ge(act_stored[m], 16 + 20 * 16)
                with act.Fori(0, 4) as c:
                    g = G_GC + c
                    hi(2, g)
                    hi(3, g)
                    hi(0, g + 1)
                    for m in range(2):
                        if m == 1:
                            hi(1, g + 1)
                        ready(m, g, g - G_IN)
                        hold(act, S.gc_done, c * 2 + (m + 1))
                        act.activation(pair(slot(m)), accv(m), ACT.Silu).then_inc(acc_free[m], 1)

                for u in range(8):
                    n = P * (u // 2 + 1)
                    act.wait_ge(S.ppeak_done, u + 1)
                    for h in range(4):
                        last = act.activation(probs_p[:, u % 2, h, 0:n], probs_p[:, u % 2, h, 0:n], ACT.Exp,
                                              bias=stat[:, 4 + h:5 + h], accum_out=stat[:, 8 + h:9 + h])
                    last.then_inc(S.exp_p, 1)
                    for k in range(u // 2 + 1):
                        f = sum(v // 2 + 1 for v in range(u)) + k
                        act.wait_ge(S.ptr_p, f + 1)
                        if f >= 2:
                            act.wait_ge(S.ptc_p, f - 1)
                        act.activation(pt_p[:, f % 2, :], aux[:, f % 2, :], ACT.Copy).then_inc(S.pv_p, 1)

                def k_copies(b):
                    for f in range(0, 8, 2):
                        hold(act, S.k_turn_a, b * 4 + (4 + f // 2 + 1))
                        act.activation(k_turned[:, f // 4, (f % 4) * 512:(f % 4) * 512 + 512], aux[:, 1, :], ACT.Copy).then_inc(S.k_cp_a, 1)

                def soft(b):
                    hold(act, S.sraw_done, b + 2)
                    act.activation(probs_s, probs_s, ACT.Exp, bias=stat[0:NS, 1:2], accum_out=stat[0:NS, 2:3]).then_inc(S.exp_s, 1)

                act.wait_ge(S.ptc_p, 20)
                k_copies(0)
                with act.Fori(0, SEQS - 1) as b:
                    k_copies(b + 1)
                    soft(b)
                soft(SEQS - 1)

                for n in range(16):
                    if n < 8:
                        act.wait_ge(S.pv_s, 1 + 8)
                        act.activation(act_hi[:, n, :], d_t[:, n, :], ACT.Copy).then_inc(S.split_hi, 1)
                    else:
                        act.wait_ge(S.ag_ready, n - 7)
                        act.activation(act_lo[:, n - 8, :], slot(4 + n % 4), ACT.Copy).then_inc(S.split_hi, 1)

                def only_splits(g0, n):
                    with act.Fori(0, n) as c:
                        hi(2, g0 + c)
                        hi(3, g0 + c)
                        hi(0, g0 + c + 1)
                        hi(1, g0 + c + 1)

                only_splits(G_MG, 8)
                for k in range(KT):
                    act.wait_ge(S.gates_used, 2 + 8)
                    act.activation(act_hi[:, k, :], xtile(k), ACT.Copy).then_inc(S.merged_hi, 1)
                only_splits(G_OUT, 7)
                hi(2, N_GROUPS - 1)
                hi(3, N_GROUPS - 1)
                for s in range(2):
                    act.wait_ge(u_stored[s], 32 + 32 * 4)
                end_of_layer(act, l + 2)
            for t, (t0, n) in enumerate(TT):
                for f in range(4):
                    i = 4 * t + f
                    act.wait_ge(y_turned, i + 1)
                    act.activation(x_rows[0:n, t, 512 * f:512 * f + 512], acc[0:n, i % 4, :], ACT.Copy).then_inc(y_copied, 1)

        @block.tensor
        def _(pe):
            pe.wait_ge(tables_in, 32)
            pe.wait_ge(rows_in, 64)
            for k in range(KT):
                if k >= 2:
                    pe.wait_ge(pro_copied, 2 * (k - 1))
                for t, (t0, n) in enumerate(TT):
                    out = acc[:, 2 * (k % 2), t0:t0 + n] if t < 4 else acc[:, 2 * (k % 2) + 1, 0:n]
                    last = pe.transpose(out, x_rows[0:n, t, k * P:(k + 1) * P], ident[0:n, 0:n])
                last.then_inc(pro_turned, 1)
            for k in range(KT):
                last = pe.transpose(aux[:, 0, 9 * k:9 * k + 9], c_rows[:, k * P:(k + 1) * P], ident[0:9, 0:9])
            last.then_inc(pro_turned, 1)
            end_of_layer(pe, 1)

            def group(g, sets, rhs=None, before=None):
                for b0, b1, a0, a1 in sets:
                    for i in range(b0, b1 + 1):
                        hold(pe, S.w_lo, 4 * g + i + 5)
                        if before:
                            pe.wait_ge(before, 4 * (i + 1))
                        for m in range(2):
                            if i == b0:
                                hold(pe, acc_free[m], (a0, a1)[m] + 1)
                            for k in range(4):
                                kt = 4 * (i - b0) + k
                                hi_r, lo_r = rhs(i, kt)
                                for n, (w, x) in enumerate(((w_hi_t, hi_r), (w_hi_t, lo_r), (w_lo_t, hi_r))):
                                    for h in range(2):
                                        last = pe.matmul(acc[:, 2 * m + h, 0:HALF], w[:, i % 2, k, P * m:P * m + P],
                                                         x[:, h * HALF:(h + 1) * HALF],
                                                         start=i == b0 and k == 0 and n == 0, stop=i == b1 and k == 3 and n == 2)
                            if i == b1 and m == 0:
                                last.then_inc(S.acc0_ready, 1)
                        last.then_inc(S.w_used, 1)

            def of_h(i, kt):
                return act_hi[:, kt, :], act_lo[:, kt, :]

            def fp32_pair(bank, lhsT, rhs):
                for h in range(2):
                    last = pe.matmul(aux[:, bank + h, 0:HALF], lhsT, rhs[:, h * HALF:(h + 1) * HALF], start=True, stop=True)
                return last

            with pe.Fori(0, DEPTH) as l:
                pe.sem_inc(S.w_used, 2)
                pe.sem_inc(S.acc0_free, 1)
                pe.sem_inc(S.acc1_free, 1)
                pe.sem_inc(S.mod_turned, 2)
                pe.sem_inc(S.k_turn_a, 4)
                pe.sem_inc(S.k_turn_b, 4)
                pe.sem_inc(S.pv_s, 1)
                pe.wait_ge(S.params_in, 160)
                pe.transpose(aux[:, 2, 0:N_PAR], par_rows[:, :], ident[0:N_PAR, 0:N_PAR])
                for j in range(CT_):
                    last = pe.transpose(aux[:, 3, TAPS * j:TAPS * (j + 1)], conv_rows[:, j * P:(j + 1) * P], ident[0:TAPS, 0:TAPS])
                last.then_inc(S.params_turned, 1)
                pe.wait_ge(S.xsum, 2 + KT)
                fp32_pair(0, ones, slot(2)).then_inc(S.ssq_x, 1)
                pe.wait_ge(S.params_done, 1)
                with pe.Fori(0, 12) as cc:
                    for s in range(2):
                        g = cc * 2 + s
                        for i in range(4):
                            hold(pe, S.w_lo, 4 * g + i + 5)
                            for k in range(4):
                                for w in (w_hi_t, w_lo_t):
                                    last = pe.matmul(acc[0:18, 2 * s, 0:256], c_split[:, 4 * i + k, :], w[:, i % 2, k, :],
                                                     start=i == 0 and k == 0 and w is w_hi_t, stop=i == 3 and k == 3 and w is w_lo_t)
                            last.then_inc(S.w_used, 1)
                        hold(pe, S.row_ready, g + 1)
                        hold(pe, S.mod_done, g + 1)
                        for a in range(2):
                            last = pe.matmul(aux[:, 2 + s, 9 * a:9 * a + 9], slot(7)[0:18, 256 * s + P * a:256 * s + P * a + P],
                                             tab[0:18, T_COMB:T_COMB + 9], start=True, stop=True)
                        last.then_inc(S.mod_turned, 1)
                pe.wait_ge(S.h_lo, 2 + KT)

                def part1(g, kinds, aux_n, js, jn):
                    a = g - G_IN
                    group(g, [(0, 3, a, a)], of_h)
                    for m, kind in enumerate(kinds):
                        if kind is None:
                            continue
                        hold(pe, acc_free[m], a + 2)
                        hold(pe, S.swap_used, js + m + 1)
                        if kind == "v":
                            for t, (t0, n) in enumerate(TT):
                                out = aux[:, 2, t0:t0 + n] if t < 4 else aux[0:n, 3, 0:P]
                                last = pe.transpose(out, slot(m)[:, t0:t0 + n], ident)
                        else:
                            sw = T_SWQ if kind == "q" else T_SWI
                            if kind != "qi":
                                hold(pe, S.std_ready, jn + m + 1)
                                fp32_pair(0, tab[:, T_ONE64:T_ONE64 + P] if kind == "ki" else ones, slot(2 + m))
                            last = fp32_pair(2, tab[:, sw:sw + P], slot(m))
                        last.then_inc(S.aux_ready, 1)

                with pe.Fori(0, 4) as c:
                    part1(G_Q + c, ("q", "q"), c * 2, c * 2, c * 2)
                part1(G_K, ("q", "q"), 8, 8, 8)
                part1(G_V, ("v", "v"), 10, 10, 10)
                with pe.Fori(0, 4) as c:
                    part1(G_QI + c, ("qi", "qi"), c * 2 + 12, c * 2 + 12, 10)
                part1(G_KI, ("ki", None), 20, 20, 10)

                pe.wait_ge(S.rope_done, 2 + 21)
                pe.wait_ge(S.acc1_free, 11 + 1)
                for t, (t0, n) in enumerate(TT):
                    main = t < 4
                    for h in range(KVH):
                        out = aux[:, h, t0:t0 + n] if main else aux[0:n, 3, P * h:P * h + P]
                        pe.transpose(out, k_new[:, h, t0:t0 + n], ident)
                    out = aux[:, 2, ID * t:ID * t + ID] if main else aux[0:n, 3, 256:256 + ID]
                    pe.transpose(out, ki_new[0:ID, t0:t0 + n], ident[0:ID, 0:ID])
                    if main:
                        pe.transpose(aux[:, 2, 256 + IH * t:256 + IH * t + IH], wi_new[:, t0:t0 + n], ident[0:IH, 0:IH])
                pe.matmul(aux[0:64, 3, 320:320 + NS], tab[0:IH, T_EXP:T_EXP + 64], wi_new[:, SEQ:TOK],
                          start=True, stop=True).then_inc(S.tok_turned, 1)

                pe.wait_ge(S.tok_done, 1)
                for u in range(4 * 8):
                    qt, j = divmod(u, 8)
                    n = P * (qt + 1)
                    if u >= 2:
                        pe.wait_ge(S.relu_done, u - 1)
                    for h in range(2):
                        last = pe.matmul(aux[:, 2 * (u % 2) + h, 0:n], d_t[64 * h:64 * h + 64, j, qt * P:qt * P + P],
                                         ki_new[64 * h:64 * h + 64, 0:n], start=True, stop=True)
                    last.then_inc(S.dots_ready, 1)

                pe.wait_ge(S.diag_done, 1)
                pe.wait_ge(S.relu_done, 32)
                pe.wait_ge(S.acc0_free, 1 + 11)

                def turn_x(f):
                    b, ch = divmod(f, 4)
                    pe.wait_ge(kx_landed[b % 2], 256 * (b // 2 + 1))
                    if f >= 1:
                        pe.wait_ge(S.kx_copied, f)
                    for g in range(2):
                        two_pages = kx_pages[:, b % 2, 4 * ch + 2 * g:4 * ch + 2 * g + 2, :].rearrange("p g n -> p (g n)")
                        last = pe.transpose(aux[:, 0, P * g:P * g + P], two_pages, ident)
                    last.then_inc(S.kx_turned_ps, 1)

                def dots_x(f):
                    pe.wait_ge(S.kx_copied, f + 1)
                    if f >= 1:
                        pe.wait_ge(S.srelu_done, f)
                    for h in range(2):
                        half = slice(64 * h, 64 * h + 64)
                        last = pe.matmul(aux[0:64, 2 + h, 0:256], qi_all[half, f // 4, :], kx_turned[half, f % 2, :], start=True, stop=True)
                    last.then_inc(S.sdots_ready, 1)

                def mix_x(f):
                    b, ch = divmod(f, 4)
                    pe.wait_ge(S.srelu_done, f + 1)
                    pe.matmul(acc[0:NS, ch, :], wi_mix[:, b, :], relu_s[:, f % 2, :], start=b == 0,
                              stop=b == SEQS - 1).then_inc(S.mixed, 1)

                NF = 4 * SEQS
                for f in range(NF + 2):
                    if f < NF:
                        turn_x(f)
                    if 1 <= f <= NF:
                        dots_x(f - 1)
                    if f >= 2:
                        mix_x(f - 2)
                pe.wait_ge(S.srelu_done, NF)
                for b in range(SEQS):
                    last = pe.matmul(aux[0:64, 2, STEPS * b:STEPS * b + STEPS], qi_all[0:64, b, :],
                                     ki_new[0:64, SEQ + STEPS * b:SEQ + STEPS * b + STEPS], start=True, stop=True)
                last.then_inc(S.sdots_ready, 1)
                pe.wait_ge(S.srelu_done, NF + 1)
                for b in range(SEQS):
                    last = pe.matmul(aux[0:NS, 1, 0:STEPS], wi_mix[:, b, :], relu_tail[:, STEPS * b:STEPS * b + STEPS],
                                     start=b == 0, stop=b == SEQS - 1)
                last.then_inc(S.mixed, 1)
                pe.wait_ge(S.score_s_done, 1)

                with pe.Fori(0, 4) as cc:
                    for s in range(2):
                        c = cc * 2 + s
                        g = G_GLU + c
                        group(g, [(0, 3, g - G_IN, g - G_IN)], of_h)
                        hold(pe, state_in[s], cc * 16 + 16)
                        hold(pe, S.state_turned, c + 1)
                        for h in range(2):
                            last = pe.transpose(aux[:, 0, 120 * h:120 * h + 120], state_rows[:, s, h, :], ident[0:120, 0:120])
                        last.then_inc(S.state_used, 1)
                        hold(pe, S.u_done, c + 3)
                        pe.transpose(aux[0:HIST, 1, 0:P], u_pad[s][:, SEQ:SEQ + HIST], ident)
                        last = pe.transpose(aux[0:NS, 1, P:2 * P], slot(s)[:, SEQ:TOK], ident)
                        last.then_inc(S.u_turned, 1)

                def plain(g0, n):
                    with pe.Fori(0, n) as c:
                        group(g0 + c, [(0, 3, g0 + c - G_IN, g0 + c - G_IN)], of_h)

                plain(G_MERGE, 4)
                pe.wait_ge(S.mean_in, 1)
                fp32_pair(0, ones, slot(7)).then_inc(S.mean_ps, 1)
                plain(G_MERGE + 4, 4)
                pe.wait_ge(S.cvar_in, CT_)
                fp32_pair(2, ones, slot(6)).then_inc(S.var_ps, 1)
                plain(G_MERGE + 8, 16)

                pe.wait_ge(S.q_back, 16)
                pe.wait_ge(S.bias_done, 1)
                pe.wait_ge(S.acc0_free, 1 + 43)
                pe.wait_ge(S.acc1_free, 1 + 43)

                def logits(u):
                    qt, g = divmod(u, KVH)
                    n = P * (qt + 1)
                    if u >= 1:
                        pe.wait_ge(S.probs_raw, u)
                    for h in range(GROUP):
                        last = pe.matmul(acc[:, h, 0:n], q_att[:, GROUP * g + h, qt * P:qt * P + P], k_new[:, g, 0:n], start=True, stop=True)
                    last.then_inc(S.logits_p, 1)

                def values(u):
                    qt, g = divmod(u, KVH)
                    f0 = sum(v // 2 + 1 for v in range(u))
                    pe.wait_ge(S.p_ready, u + 1)
                    if u >= 2:
                        pe.wait_ge(S.ao_p, u - 1)

                    def turn(k):
                        if f0 + k >= 2:
                            pe.wait_ge(S.pv_p, f0 + k - 1)
                        for h in range(GROUP):
                            last = pe.transpose(aux[:, (f0 + k) % 2, P * h:P * h + P], probs_p[:, u % 2, h, k * P:k * P + P], ident)
                        last.then_inc(S.ptr_p, 1)

                    turn(0)
                    for k in range(qt + 1):
                        if k < qt:
                            turn(k + 1)
                        pe.wait_ge(S.pv_p, f0 + k + 1)
                        pe.matmul(aux[:, 2 + u % 2, :], v_tok[:, k, g * HD:(g + 1) * HD], pt_p[:, (f0 + k) % 2, :],
                                  start=k == 0, stop=k == qt).then_inc(S.ptc_p, 1)

                logits(0)
                for u in range(8):
                    if u < 7:
                        logits(u + 1)
                    values(u)
                pe.wait_ge(S.ao_p, 8)

                def turn_k(b):
                    hold(pe, S.k_landed, b * 256 + 256)
                    for f in range(8):
                        bank, done, ready_ = (1, S.k_cp_a, S.k_turn_a) if f % 2 == 0 else (2, S.k_cp_b, S.k_turn_b)
                        if f >= 2:
                            hold(pe, done, b * 4 + (f // 2 + 1))
                        for g in range(4):
                            last = pe.transpose(aux[:, bank, P * g:P * g + P],
                                                k_pages[:, 4 * (f % 4) + g, (f // 4) * HD:(f // 4) * HD + HD], ident)
                        last.then_inc(ready_, 1)

                def sample_logits(b):
                    hold(pe, S.k_cp_a, b * 4 + 5)
                    hold(pe, S.k_cp_b, b * 4 + 5)
                    hold(pe, S.q_one_done, b + 1)
                    hold(pe, S.sraw_done, b + 1)
                    for ch in range(5):
                        for g in range(KVH):
                            n = 512 if ch < 4 else STEPS
                            out = acc[0:NS, ch, 0:n] if ch < 4 else aux[0:NS, 0, 0:n]
                            last = pe.matmul(out, q_one[:, g, :], k_turned[:, g, ch * 512:ch * 512 + n], start=g == 0, stop=g == 1)
                    last.then_inc(S.logits_s, 1)

                def sample_values(b):
                    hold(pe, S.ps_ready, b + 1)
                    for k in range(PAGES):
                        pe.transpose(aux[:, 1, NS * k:NS * k + NS], probs_s[:, k * P:k * P + P], ident[0:NS, 0:NS])
                    pe.transpose(aux[0:NS, 2, 0:NS], p_tail, ident[0:NS, 0:NS]).then_inc(S.pts_ps, 1)
                    hold(pe, S.v_landed, b * 256 + 256)
                    hold(pe, S.pts_done, b + 1)
                    for g in range(KVH):
                        for k in range(PAGES + 1):
                            v = v_pages[:, k, g * HD:(g + 1) * HD] if k < PAGES else v_tok[0:NS, 4, g * HD:(g + 1) * HD]
                            p = p_turned[:, k, 16 * g:16 * g + 16] if k < PAGES else p_turned[0:NS, k, 16 * g:16 * g + 16]
                            last = pe.matmul(aux[:, 3, 16 * g:16 * g + 16], v, p, start=k == 0, stop=k == PAGES)
                    last.then_inc(S.pv_s, 1)

                turn_k(0)
                with pe.Fori(0, SEQS - 1) as b:
                    sample_logits(b)
                    turn_k(b + 1)
                    hold(pe, S.k_cp_a, b * 4 + 9)
                    hold(pe, S.k_cp_b, b * 4 + 9)
                    sample_values(b)
                    hold(pe, S.pts_done, b + 1)
                sample_logits(SEQS - 1)
                sample_values(SEQS - 1)

                pe.wait_ge(S.split_lo, 16)
                with pe.Fori(0, 8) as c:
                    group(G_MG + c, [(0, 1, c * 2 + 43, c * 2 + 43), (2, 3, c * 2 + 44, c * 2 + 44)],
                          lambda i, kt: (act_lo[:, kt, :], act_lo[:, 8 + kt, :]) if i < 2 else (act_hi[:, kt, :], act_hi[:, 8 + kt, :]))
                with pe.Fori(0, 8) as c:
                    group(G_OUT + c, [(0, 3, c + 59, c + 59)], of_h, before=S.merged_lo)
                end_of_layer(pe, l + 2)
            for t, (t0, n) in enumerate(TT):
                for f in range(4):
                    i = 4 * t + f
                    if i >= 4:
                        pe.wait_ge(y_copied, i - 3)
                    for k in range(4):
                        last = pe.transpose(acc[0:n, i % 4, P * k:P * k + P], x_v[:, 4 * f + k, t0:t0 + n], ident)
                    last.then_inc(y_turned, 1)

        @block.vector
        def _(dve):
            dve.memset(eps[:, :], EPS).then_inc(eps_set, 1)
            dve.wait_ge(pro_c, 2)
            dve.tensor_tensor(c_split[:, :, 9:18], slot(0)[:, 0:144].rearrange("p (k n) -> p k n", n=9),
                              c_split[:, :, 0:9].bitcast(F32), ALU.subtract).then_inc(pro_c, 1)
            dve.wait_ge(pro_c, 3)
            end_of_layer(dve, 1)
            st = Steps(dve, S.dve)

            def bc(ap, n):
                return ap.unsqueeze(2).to_broadcast([ap.shape[0], ap.shape[1], n])

            with dve.Fori(0, DEPTH) as l:
                dve.sem_inc(S.rope_done, 2)
                dve.sem_inc(S.swap_used, 1)
                dve.sem_inc(S.std_ready, 1)
                dve.sem_inc(S.mod_done, 1)
                dve.memset(slot(2), 0.0).then_inc(S.xsum, 2)
                dve.wait_ge(S.params_turned, 1)
                st.then(dve.tensor_copy(par[:, :], aux[:, 2, 0:N_PAR]))
                dve.tensor_copy(cw[:, :, :].rearrange("p j k -> p (j k)"), aux[:, 3, 0:CT_ * TAPS]).then_inc(S.params_done, 1)
                with dve.Fori(0, KT // 2) as kk:
                    for s in range(2):
                        kt = kk * 2 + s
                        hold(dve, S.sq_ready, kt + 1)
                        hold(dve, S.xsum, kt + 2)
                        dve.tensor_tensor(slot(2), slot(2), slot(s), ALU.add).then_inc(S.xsum, 1)
                st.close()
                with dve.Fori(0, 12) as cc:
                    for s in range(2):
                        g = cc * 2 + s
                        hold(dve, S.mod_turned, g + 3)
                        dve.tensor_tensor(mod[:, ds(g * 2, 2), :], aux[:, 2 + s, 0:18].rearrange("p (a n) -> p a n", n=9),
                                          bc(par[:, ds(g * 2 + R_BADA, 2)], 9), ALU.add).then_inc(S.mod_done, 1)
                dve.wait_ge(S.mod_done, 1 + 24)
                st.then(dve.scalar_tensor_tensor(out=mod[:, 16:32, :], in0=mod[:, 16:32, :], scalar=1.0,
                                                 in1=bc(par[:, R_NORM:R_NORM + KT], 9), op0=ALU.add, op1=ALU.mult))
                dve.wait_ge(S.rstd_x, 1)
                st.then(dve.reciprocal(slot(3), slot(3)))
                st.close()
                with dve.Fori(0, KT // 2) as kk:
                    for s in range(2):
                        kt = kk * 2 + s
                        gain, shift = mod[:, ds(kt + 16, 1), :].rearrange("p a n -> p (a n)"), mod[:, ds(kt, 1), :].rearrange("p a n -> p (a n)")
                        st.then(dve.tensor_tensor(slot(2), xtile(kt), slot(3), ALU.mult))
                        st.wait()
                        hold(dve, S.h_lo, kt + 1)
                        st.then(dve.tensor_scalar(slot(4 + s)[:, 0:SEQ], slot(2)[:, 0:SEQ], gain[:, 0:1], shift[:, 0:1], ALU.mult, ALU.add))
                        st.then(dve.tensor_tensor(samp(slot(4 + s)[:, SEQ:TOK]), samp(slot(2)[:, SEQ:TOK]), bc(gain[:, 1:9], STEPS), ALU.mult))
                        st.close()
                        dve.tensor_tensor(samp(slot(4 + s)[:, SEQ:TOK]), samp(slot(4 + s)[:, SEQ:TOK]), bc(shift[:, 1:9], STEPS),
                                          ALU.add).then_inc(S.h_ready, 1)

                def rope(m, aux_n, jn, cos, sin, out, rows=P):
                    hold(dve, S.aux_ready, aux_n + 1)
                    e = pair(slot(6 + m))
                    dve.tensor_tensor(e, aux[:, 2:4, 0:HALF], tabv(sin), ALU.mult).then_inc(S.swap_used, 1)
                    st.then(dve.tensor_tensor(slot(m), slot(m), tab[:, cos:cos + TOK], ALU.mult))
                    st.wait()
                    if jn is None:
                        dve.tensor_tensor(out, slot(6 + m), slot(m), ALU.add).then_inc(S.rope_done, 1)
                        st.close()
                        return
                    st.then(dve.tensor_tensor(slot(6 + m), slot(6 + m), slot(m), ALU.add))
                    hold(dve, S.std_ready, jn + 2)
                    st.then(dve.reciprocal(slot(4 + m), slot(4 + m)))
                    st.close()
                    dve.tensor_tensor(out, slot(6 + m), slot(4 + m), ALU.mult).then_inc(S.rope_done, 1)

                with dve.Fori(0, 4) as c:
                    for m in range(2):
                        rope(m, c * 2 + m, c * 2 + m, T_CQ, T_SQ, xtile(c * 2 + m))
                for m in range(2):
                    rope(m, 8 + m, 8 + m, T_CQ, T_SQ, k_new[:, m, :])
                for m in range(2):
                    dve.wait_ge(S.aux_ready, 11 + m)
                    dve.tensor_copy(v_tok[:, 0:4, m * HD:(m + 1) * HD], aux[:, 2, :].rearrange("p (t d) -> p t d", t=4)).then_inc(S.rope_done, 1)
                    dve.tensor_copy(v_tok[0:NS, 4, m * HD:(m + 1) * HD], aux[0:NS, 3, 0:P]).then_inc(S.swap_used, 1)
                with dve.Fori(0, 4) as c:
                    for m in range(2):
                        rope(m, c * 2 + (12 + m), None, T_CI, T_SI, d_t[:, ds(c * 2 + m, 1), :].rearrange("p a n -> p (a n)"))
                rope(0, 20, 10, T_CI, T_SI, ki_new[:, :])

                dve.wait_ge(S.tok_turned, 1)
                dve.wait_ge(S.swap_used, 1 + 21)
                for h in range(KVH):
                    st.then(dve.tensor_copy(k_tok[:, 0:4, h * HD:(h + 1) * HD], aux[:, h, :].rearrange("p (t d) -> p t d", t=4)))
                st.then(dve.tensor_copy(ki_tok[:, 0:4, :], aux[:, 2, 0:256].rearrange("p (t d) -> p t d", t=4)))
                st.then(dve.tensor_copy(wi_tok[:, :, :], aux[:, 2, 256:320].rearrange("p (t d) -> p t d", t=4)))
                st.then(dve.tensor_copy(k_tok[0:NS, 4, :], aux[0:NS, 3, 0:256]))
                st.then(dve.tensor_copy(ki_tok[0:NS, 4, :], aux[0:NS, 3, 256:320]))
                mixin = aux[0:64, 3, 320:320 + NS].unsqueeze(1).to_broadcast([64, SEQS, NS])
                dve.tensor_tensor(wi_mix[:, :, :], mixin, tab[0:64, T_MASK:T_MASK + SEQS * NS].rearrange("p (b n) -> p b n", b=SEQS),
                                  ALU.mult).then_inc(S.tok_done, 1)
                for half in range(2):
                    for h in range(2):
                        src = d_t[64 * h:64 * h + 64, :, SEQ:TOK].rearrange("p j (b t) -> p b j t", t=STEPS)
                        dst = qi_all[64 * half:64 * half + 64, :, 32 * h:32 * h + 32].rearrange("p b (j t) -> p b j t", t=STEPS)
                        last = dve.tensor_copy(dst, src)
                last.then_inc(S.diag_done, 1)

                for u in range(4 * 8):
                    qt, j = divmod(u, 8)
                    n = P * (qt + 1)
                    score = bias_p[:, qoff[qt]:qoff[qt] + n]
                    dve.wait_ge(S.relu_done, u + 1)
                    w = [wi_tok[:, qt, 2 * j + h:2 * j + h + 1] for h in range(2)]
                    if j == 0:
                        st.then(dve.tensor_scalar(score, relu_p[:, u % 2, 0, 0:n], w[0], None, ALU.mult))
                    else:
                        st.then(dve.scalar_tensor_tensor(out=score, in0=relu_p[:, u % 2, 0, 0:n], scalar=w[0], in1=score,
                                                         op0=ALU.mult, op1=ALU.add))
                    st.close()
                    dve.scalar_tensor_tensor(out=score, in0=relu_p[:, u % 2, 1, 0:n], scalar=w[1], in1=score,
                                             op0=ALU.mult, op1=ALU.add).then_inc(S.score_done, 1)
                    dve.wait_ge(S.score_done, u + 1)
                    if j == 7:
                        d = score[:, qt * P:qt * P + P]
                        st.then(dve.tensor_tensor(d, d, tab[:, T_TRI:T_TRI + P], ALU.min))
                st.close()
                for f in range(4 * SEQS):
                    dve.wait_ge(S.sdots_ready, f + 1)
                    if f >= 2:
                        dve.wait_ge(S.mixed, f - 1)
                    dve.tensor_scalar(relu_s[:, f % 2, :].rearrange("p (g h n) -> p h g n", g=2, h=2),
                                      aux[0:64, 2:4, 0:256].rearrange("p h (g n) -> p h g n", g=2), 0.0, None, ALU.max).then_inc(S.srelu_done, 1)
                dve.wait_ge(S.sdots_ready, 4 * SEQS + 1)
                dve.tensor_scalar(relu_tail, aux[0:64, 2, 0:NS], 0.0, None, ALU.max).then_inc(S.srelu_done, 1)
                dve.wait_ge(S.mixed, 4 * SEQS + 1)
                st.then(dve.tensor_copy(bias_s[:, 0:PAST].rearrange("p (c n) -> p c n", c=4), acc[0:NS, :, :]))
                dve.tensor_tensor(bias_s[:, PAST:NKEY], aux[0:NS, 1, 0:STEPS], tab[0:NS, T_UMS:T_UMS + STEPS], ALU.min).then_inc(S.score_s_done, 1)
                dve.wait_ge(S.score_s_done, 1)
                st.close()

                dve.sem_inc(S.u_done, 2)
                dve.sem_inc(S.state_turned, 1)
                dve.sem_inc(S.state_used, 2)
                dve.sem_inc(S.gc_done, 2)
                for s in range(2):
                    st.then(dve.memset(u_pad[s][:, 0:HIST], 0.0))
                st.close()
                with dve.Fori(0, 4) as cc:
                    for s in range(2):
                        c = cc * 2 + s
                        u = u_pad[s]
                        us = u[:, SEQ + HIST:UB].rearrange("p (b k) -> p b k", b=SEQS)
                        hold(dve, S.state_used, c + 3)
                        dve.tensor_copy(us[:, :, 0:HIST], aux[:, 0, 0:240].rearrange("p (b k) -> p b k", b=SEQS)).then_inc(S.state_turned, 1)
                        hold(dve, S.state_turned, c + 2)
                        a0 = G_GLU - G_IN
                        hold(dve, S.acc0_free, c + (a0 + 2))
                        hold(dve, S.acc1_free, c + (a0 + 2))
                        st.then(dve.tensor_tensor(u[:, HIST:HIST + SEQ], slot(s)[:, 0:SEQ], slot(2 + s)[:, 0:SEQ], ALU.mult))
                        st.then(dve.tensor_tensor(slot(s)[:, SEQ:TOK], slot(s)[:, SEQ:TOK], slot(2 + s)[:, SEQ:TOK], ALU.mult))
                        st.wait()
                        dve.tensor_copy(us[:, :, HIST:HIST + STEPS], samp(slot(s)[:, SEQ:TOK])).then_inc(S.u_done, 1)
                        hold(dve, S.u_done, c + 3)
                        st.close()
                        d = d_t[:, ds(c, 1), :].rearrange("p a n -> p (a n)")
                        dp, dd = d[:, 0:SEQ], samp(d[:, SEQ:TOK])
                        w = cw[:, ds(c, 1), :].rearrange("p a k -> p (a k)")
                        b = par[:, ds(c + R_CB, 1)]
                        st.then(dve.tensor_scalar(dp, u[:, 0:SEQ], w[:, 0:1], b, ALU.mult, ALU.add))
                        st.then(dve.tensor_scalar(dd, us[:, :, 0:STEPS], w[:, 0:1], b, ALU.mult, ALU.add))
                        for k in range(1, TAPS):
                            for out, src in ((dp, u[:, k:k + SEQ]), (dd, us[:, :, k:k + STEPS])):
                                st.wait(back=1)
                                st.then(dve.scalar_tensor_tensor(out=out, in0=src, scalar=w[:, k:k + 1], in1=out, op0=ALU.mult, op1=ALU.add))
                        st.close()
                st.then(dve.tensor_tensor(slot(7), d_t[:, 0, :], d_t[:, 1, :], ALU.add))
                for j in range(2, CT_):
                    st.wait()
                    ins = dve.tensor_tensor(slot(7), slot(7), d_t[:, j, :], ALU.add)
                    st.then(ins) if j < CT_ - 1 else ins.then_inc(S.mean_in, 1)
                st.close()

                def best(work, scores, m8, rounds, first=False):
                    if first:
                        st.then(dve.max(m8, scores))
                        st.wait()
                        st.then(dve.match_replace(work, m8, scores, NEG))
                        st.close()
                    with dve.Fori(0, rounds) as _r:
                        st.then(dve.max(m8, work))
                        st.wait()
                        st.then(dve.match_replace(work, m8, work, NEG))
                        st.close()

                def as_bias(work, scores):
                    st.then(dve.tensor_tensor(scores, work, scores, ALU.is_equal))
                    st.wait()
                    st.then(dve.tensor_scalar(scores, scores, -BIG, None, ALU.mult))

                dve.wait_ge(S.q_spilled, 16)
                for qt in range(1, QT):
                    sl = slice(qoff[qt], qoff[qt] + P * (qt + 1))
                    best(work_p[:, sl], bias_p[:, sl], top8[:, :], TOPK_P // 8 - 1, first=True)
                    as_bias(work_p[:, sl], bias_p[:, sl])
                st.close()
                dve.wait_ge(S.mean_done, 1)
                for j in range(CT_):
                    dve.tensor_tensor(d_t[:, j, :], d_t[:, j, :], slot(2), ALU.subtract).then_inc(S.cent_done, 1)
                for j in range(CT_):
                    dve.wait_ge(S.csq_done, j + 1)
                    if j == 0:
                        dve.tensor_copy(slot(6), slot(4)).then_inc(S.cvar_in, 1)
                    else:
                        dve.wait_ge(S.cvar_in, j)
                        dve.tensor_tensor(slot(6), slot(6), slot(4 + j % 2), ALU.add).then_inc(S.cvar_in, 1)
                best(work_s, bias_s, top8[0:NS, :], 15, first=True)
                dve.wait_ge(S.cstd_done, 1)
                st.then(dve.reciprocal(slot(3), slot(3)))
                st.close()
                for j in range(CT_):
                    dve.tensor_tensor(d_t[:, j, :], d_t[:, j, :], slot(3), ALU.mult).then_inc(S.ln_done, 1)
                best(work_s, bias_s, top8[0:NS, :], TOPK_S // 8 - 16)
                as_bias(work_s, bias_s)
                st.close()
                st.then(dve.tensor_copy(bias_p[:, 0:P], tab[:, T_TRIB:T_TRIB + P]))
                st.wait()
                dve.sem_inc(S.bias_done, 1)
                st.close()
                dve.wait_ge(S.silu_done, CT_)
                with dve.Fori(0, 4) as c:
                    for m in range(2):
                        d = d_t[:, ds(c * 2 + m, 1), :].rearrange("p a n -> p (a n)")
                        hold(dve, acc_free[m], c + (G_GC - G_IN + 2))
                        dve.tensor_tensor(d, d, slot(m), ALU.mult).then_inc(S.gc_done, 1)

                dve.wait_ge(S.gc_done, 2 + 8)
                for u in range(8):
                    qt, g = divmod(u, KVH)
                    n = P * (qt + 1)
                    dve.wait_ge(S.logits_p, u + 1)
                    if u >= 2:
                        f = sum(v // 2 + 1 for v in range(u - 1))
                        dve.wait_ge(S.ptr_p, f)
                    bias = bias_p[:, qoff[qt]:qoff[qt] + n]
                    for h in range(GROUP):
                        ins = dve.tensor_tensor_reduce(out=probs_p[:, u % 2, h, 0:n], in0=acc[:, h, 0:n], in1=bias, scale=HD ** -0.5,
                                                       scalar=NEG, op0=ALU.add, op1=ALU.max, accum_out=stat[:, h:h + 1])
                    ins.then_inc(S.probs_raw, 1)
                    dve.wait_ge(S.probs_raw, u + 1)
                    dve.tensor_scalar(stat[:, 4:8], stat[:, 0:4], -1.0, None, ALU.mult).then_inc(S.ppeak_done, 1)
                    dve.wait_ge(S.exp_p, u + 1)
                    st.then(dve.reciprocal(stat[:, 12:16], stat[:, 8:12]))
                    st.close()
                    for h in range(GROUP):
                        ins = dve.tensor_scalar(probs_p[:, u % 2, h, 0:n], probs_p[:, u % 2, h, 0:n], stat[:, 12 + h:13 + h], None, ALU.mult)
                    ins.then_inc(S.p_ready, 1)
                    if u >= 1:
                        qb, gb = divmod(u - 1, KVH)
                        dve.wait_ge(S.ptc_p, sum(v // 2 + 1 for v in range(u)))
                        dve.tensor_copy(attn_o[:, GROUP * gb:GROUP * gb + GROUP, qb * P:qb * P + P],
                                        aux[:, 2 + (u - 1) % 2, :].rearrange("p (h n) -> p h n", h=GROUP)).then_inc(S.ao_p, 1)
                dve.wait_ge(S.ptc_p, 20)
                dve.tensor_copy(attn_o[:, GROUP:HEADS, 3 * P:4 * P], aux[:, 3, :].rearrange("p (h n) -> p h n", h=GROUP)).then_inc(S.ao_p, 1)

                dve.sem_inc(S.sraw_done, 1)
                dve.sem_inc(S.k_cp_b, 1)
                dve.sem_inc(S.k_cp_a, 1)
                st.then(dve.memset(q_one[:, :, :], 0.0))
                st.close()

                def k_copies(b):
                    for g in range(KVH):
                        st.then(dve.tensor_copy(q_one[:, g, 16 * g:16 * g + 16].rearrange("p (j t) -> p j t", t=STEPS),
                                                q_att[:, GROUP * g:GROUP * g + GROUP, ds(b * STEPS + SEQ, STEPS)]))
                    dve.tensor_copy(k_turned[:, :, PAST:NKEY], k_new[:, :, ds(b * STEPS + SEQ, STEPS)]).then_inc(S.q_one_done, 1)
                    for f in range(1, 8, 2):
                        hold(dve, S.k_turn_b, b * 4 + (4 + f // 2 + 1))
                        dve.tensor_copy(k_turned[:, f // 4, (f % 4) * 512:(f % 4) * 512 + 512], aux[:, 2, :]).then_inc(S.k_cp_b, 1)
                    st.close()

                def soft1(b):
                    hold(dve, S.logits_s, b + 1)
                    hold(dve, S.brep_in, b * 128 + 128)
                    st.then(dve.tensor_tensor_reduce(out=probs_s[:, 0:PAST], in0=acc[0:NS, :, :].rearrange("p c n -> p (c n)"),
                                                     in1=bias_rep[:, 0:PAST], scale=HD ** -0.5, scalar=NEG, op0=ALU.add, op1=ALU.max,
                                                     accum_out=stat[0:NS, 0:1]))
                    st.then(dve.tensor_tensor_reduce(out=probs_s[:, PAST:NKEY], in0=aux[0:NS, 0, 0:STEPS], in1=bias_rep[:, PAST:NKEY],
                                                     scale=HD ** -0.5, scalar=NEG, op0=ALU.add, op1=ALU.max, accum_out=stat[0:NS, 3:4]))
                    st.close()
                    dve.tensor_scalar(stat[0:NS, 1:2], stat[0:NS, 0:1], stat[0:NS, 3:4], -1.0, ALU.max, ALU.mult).then_inc(S.sraw_done, 1)

                def soft2(b):
                    hold(dve, S.exp_s, b + 1)
                    st.then(dve.reciprocal(stat[0:NS, 12:13], stat[0:NS, 2:3]))
                    st.then(dve.memset(p_tail, 0.0))
                    st.wait()
                    st.then(dve.tensor_scalar(probs_s, probs_s, stat[0:NS, 12:13], None, ALU.mult))
                    st.close()
                    dve.tensor_copy(p_tail[:, ds(b * STEPS, STEPS)], probs_s[:, PAST:NKEY]).then_inc(S.ps_ready, 1)
                    hold(dve, S.pts_ps, b + 1)
                    st.then(dve.tensor_copy(p_turned[:, 0:PAGES, :].rearrange("p k n -> p (k n)"), aux[:, 1, :]))
                    dve.tensor_copy(p_turned[0:NS, PAGES, :], aux[0:NS, 2, 0:NS]).then_inc(S.pts_done, 1)
                    st.close()
                    hold(dve, S.pv_s, b + 2)
                    dve.tensor_copy(attn_o[:, 0:HEADS, ds(b * STEPS + SEQ, STEPS)],
                                    aux[:, 3, 0:32].rearrange("p (h t) -> p h t", t=STEPS)).then_inc(S.ao_s, 1)

                k_copies(0)
                with dve.Fori(0, SEQS - 1) as b:
                    soft1(b)
                    k_copies(b + 1)
                    soft2(b)
                soft1(SEQS - 1)
                soft2(SEQS - 1)

                for h in range(HEADS):
                    dve.wait_ge(ga_in[h % 4], 16 * (h // 4 + 1))
                    if h >= 4:
                        dve.wait_ge(S.split_lo, 8 + h - 3)
                    dve.wait_ge(S.ao_s, 8)
                    dve.tensor_tensor(slot(4 + h % 4), attn_o[:, h, :], slot(h % 4), ALU.mult).then_inc(S.ag_ready, 1)

                dve.sem_inc(S.gates_used, 2)
                with dve.Fori(0, 4) as cc:
                    for s in range(2):
                        c = cc * 2 + s
                        g = G_MG + c
                        hold(dve, gates_in[s], cc * 32 + 32)
                        hold(dve, S.acc0_ready, c * 2 + (43 + 1))
                        dve.tensor_tensor(pair(xtile(c * 2)), accv(0), pair(slot(4 * s)), ALU.mult).then_inc(acc_free[0], 1)
                        hold(dve, S.w_used, 4 * g + (2 + 2))
                        dve.tensor_tensor(pair(xtile(c * 2 + 1)), accv(1), pair(slot(4 * s + 1)), ALU.mult).then_inc(acc_free[1], 1)
                        hold(dve, S.acc0_ready, c * 2 + (43 + 2))
                        dve.tensor_tensor(pair(slot(4 * s + 2)), accv(0), pair(slot(4 * s + 2)), ALU.mult).then_inc(acc_free[0], 1)
                        hold(dve, acc_free[0], c * 2 + (43 + 2 + 1))
                        st.then(dve.tensor_tensor(xtile(c * 2), xtile(c * 2), slot(4 * s + 2), ALU.add))
                        hold(dve, S.w_used, 4 * g + (4 + 2))
                        dve.tensor_tensor(pair(slot(4 * s + 3)), accv(1), pair(slot(4 * s + 3)), ALU.mult).then_inc(acc_free[1], 1)
                        hold(dve, acc_free[1], c * 2 + (43 + 2 + 1))
                        st.close()
                        dve.tensor_tensor(xtile(c * 2 + 1), xtile(c * 2 + 1), slot(4 * s + 3), ALU.add).then_inc(S.gates_used, 1)

                dve.sem_inc(S.x_new_done, 4)
                dve.wait_ge(S.merged_lo, 16)
                with dve.Fori(0, 4) as cc:
                    for s in range(2):
                        c = cc * 2 + s
                        g = G_OUT + c
                        hold(dve, x_old_in[s], cc * 16 + 16)
                        for m in range(2):
                            if m == 0:
                                hold(dve, S.acc0_ready, c + (59 + 1))
                            else:
                                hold(dve, S.w_used, 4 * g + 6)
                            k = c * 2 + m
                            gate = mod[:, ds(k + 32, 1), :].rearrange("p a n -> p (a n)")
                            old = slot(2 * s + m)
                            st.then(dve.scalar_tensor_tensor(out=pair(xtile(k)), in0=accv(m), scalar=gate[:, 0:1], in1=pair(old),
                                                             op0=ALU.mult, op1=ALU.add))
                            dve.tensor_tensor(samp(slot(4 + 2 * s + m)[:, 0:NS]), samp(acc[:, 2 * m + 1, HALF - NS:HALF]), bc(gate[:, 1:9], STEPS),
                                              ALU.mult).then_inc(acc_free[m], 1)
                            hold(dve, acc_free[m], c + (59 + 2))
                            st.close()
                            xs = x_t[:, ds(k * TOK + SEQ, NS)]
                            dve.tensor_tensor(xs, slot(4 + 2 * s + m)[:, 0:NS], old[:, SEQ:TOK], ALU.add).then_inc(S.x_new_done, 1)
                end_of_layer(dve, l + 2)


_INS = ['x_prompt', 'x_sample', 'c_prompt', 'c_sample', 'cache_k', 'cache_v', 'cache_kidx', 'state_conv', 'page_table',
        'norm_g', 'w_ada', 'b_ada', 'w_in', 'q_norm_g', 'k_norm_g', 'idx_k_norm_g', 'conv_w', 'conv_b', 'conv_ln_g',
        'conv_ln_b', 'w_attn_out', 'w_conv_out', 'w_out']
_OUTS = [(1, SEQ, DM), (SEQS, STEPS, DM), (DEPTH, 1, SEQ, KVH, HD), (DEPTH, 1, SEQ, KVH, HD), (DEPTH, 1, SEQ, ID),
         (DEPTH, 1, HIST, CW_), (DEPTH, SEQS, STEPS, KVH, HD), (DEPTH, SEQS, STEPS, KVH, HD), (DEPTH, SEQS, STEPS, ID),
         (DEPTH, SEQS, HIST, CW_)]


def kernel(**inputs):
    import numpy as _np
    import concourse.bacc as _bacc
    from concourse import mybir as _mybir
    from concourse.bass_utils import run_bass_kernel_spmd as _run

    nc = _bacc.Bacc("TRN2", target_bir_lowering=False, num_devices=1)
    arrays, args = {}, []
    for name in _INS:
        a = _np.ascontiguousarray(inputs[name])
        arrays[f"in_{name}_dram"] = a
        args.append(nc.dram_tensor(f"in_{name}_dram", a.shape, _mybir.dt.from_np(a.dtype), kind="ExternalInput").ap())
    t = tables()
    arrays["in_table_dram"] = t
    args.append(nc.dram_tensor("in_table_dram", t.shape, _mybir.dt.from_np(t.dtype), kind="ExternalInput").ap())
    for i, shape in enumerate(_OUTS):
        args.append(nc.dram_tensor(f"out_{i}_dram", shape, _mybir.dt.float32, kind="ExternalOutput").ap())
    trunk_kernel(nc, *args)
    r = _run(nc, [arrays], core_ids=[0])
    return tuple(r.results[0][f"out_{i}_dram"] for i in range(len(_OUTS)))
```

```python
from contextlib import ExitStack

import concourse.bass as bass
from concourse import mybir

F32 = mybir.dt.float32
F32R = mybir.dt.float32r
I32 = mybir.dt.int32
ACT = mybir.ActivationFunctionType
ALU = mybir.AluOpType
AX_X = mybir.AxisListType.X
ds = bass.ds

P = 128
DEPTH, DM, SEQ, SEQS, STEPS = 2, 2048, 512, 8, 4
NS = SEQS * STEPS
TOK = SEQ + NS
HALF = TOK // 2
KT = DM // P
PAST, PAGE = 2048, 128
PAGES = PAST // PAGE
NKEY = PAST + STEPS
HEADS, HD, KVH, IH, ID = 8, 128, 2, 16, 64
GROUP = HEADS // KVH
ATT, KVW, CW_, TAPS = HEADS * HD, KVH * HD, DM // 2, 31
HIST = TAPS - 1
TOPK_P = min(256, SEQ // 4)
TOPK_S = min(256, NKEY // 4)
EPS = 1e-6
NEG = -3.0e38
BIG = 1.0e30
QT = SEQ // P
CT_ = CW_ // P

C_Q = 0
C_K = C_Q + ATT
C_V = C_K + KVW
C_QI = C_V + KVW
C_KI = C_QI + IH * ID
C_WI = C_KI + ID
C_GA = C_WI + IH
C_GLU = C_GA + ATT
C_GC = C_GLU + 2 * CW_
C_MG = C_GC + CW_

G_ADA, G_IN, G_MG, G_OUT = 0, 24, 67, 75
G_Q, G_K, G_V, G_QI, G_KI = 24, 28, 29, 30, 34
G_GLU, G_MERGE, G_GA, G_GC = 35, 43, 59, 63
N_GROUPS = 83

R_NORM, R_BADA, R_QG, R_KG, R_IG, R_CB, R_LG, R_LB, N_PAR = 0, 16, 64, 65, 66, 67, 75, 83, 91

T_ID, T_ONE, T_ONE64, T_SWQ, T_SWI = 0, 128, 256, 384, 512
T_CQ, T_SQ, T_CI, T_SI = 640, 640 + TOK, 640 + 2 * TOK, 640 + 3 * TOK
T_TRI = 640 + 4 * TOK
T_TRIB = T_TRI + 128
T_UMS = T_TRIB + 128
T_COMB = T_UMS + STEPS
T_EXP = T_COMB + 9
T_MASK = T_EXP + 64
N_TAB = T_MASK + SEQS * NS


def tables():
    import numpy as np

    t = np.zeros((P, N_TAB), np.float32)
    t[:, T_ID:T_ID + P] = np.eye(P)
    t[:, T_ONE:T_ONE + P] = 1.0
    for a in range(2):
        t[64 * a:64 * a + 64, T_ONE64 + 64 * a:T_ONE64 + 64 * a + 64] = 1.0
    pos = np.concatenate([np.arange(SEQ), np.tile(PAST + np.arange(STEPS), SEQS)]).astype(np.float32)
    for dim, swap, cos, sin in ((HD, T_SWQ, T_CQ, T_SQ), (ID, T_SWI, T_CI, T_SI)):
        half = dim // 8
        inv = np.float32(500000.0) ** (-(np.arange(half, dtype=np.float32) / np.float32(half)))
        ang = (pos[:, None] * inv[None, :].astype(np.float32)).astype(np.float32)
        c, s = np.cos(ang).T, np.sin(ang).T
        t[:, cos:cos + TOK] = 1.0
        for r in range(0, P, dim):
            t[r:r + half, cos:cos + TOK] = c
            t[r + half:r + 2 * half, cos:cos + TOK] = c
            t[r:r + half, sin:sin + TOK] = -s
            t[r + half:r + 2 * half, sin:sin + TOK] = s
            for d in range(half):
                t[r + d + half, swap + r + d] = 1.0
                t[r + d, swap + r + d + half] = 1.0
    q, k = np.arange(P)[:, None], np.arange(P)[None, :]
    t[:, T_TRI:T_TRI + P] = np.where(k <= q, 3.4e38, NEG)
    t[:, T_TRIB:T_TRIB + P] = np.where(k <= q, 0.0, -BIG)
    r = np.arange(NS)
    t[:NS, T_UMS:T_UMS + STEPS] = np.where(np.arange(STEPS)[None, :] <= (r % STEPS)[:, None], 3.4e38, NEG)
    for a in range(2):
        t[9 * a:9 * a + 9, T_COMB:T_COMB + 9] = np.eye(9)
    for h in range(IH):
        for s in range(STEPS):
            t[h, T_EXP + 32 * (h % 2) + STEPS * (h // 2) + s] = 1.0
    for row in range(64):
        for b in range(SEQS):
            t[row, T_MASK + b * NS + STEPS * b + row % STEPS] = 1.0
    return t


def trunk_kernel(nc, x_prompt, x_sample, c_prompt, c_sample, cache_k, cache_v, cache_kidx, state_conv, page_table,
                 norm_g, w_ada, b_ada, w_in, q_norm_g, k_norm_g, idx_k_norm_g, conv_w, conv_b, conv_ln_g, conv_ln_b,
                 w_attn_out, w_conv_out, w_out, table,
                 y_prompt, y_sample, k_prompt, v_prompt, ki_prompt, cv_prompt, k_sample, v_sample, ki_sample, cv_sample):
    n_phys = cache_k.shape[1]
    with ExitStack() as ctx:
        def sb(name, shape, dt=F32):
            return ctx.enter_context(nc.sbuf_tensor(name, shape, dt))

        x_spill = nc.dram_tensor("x_spill", [P, KT, TOK], F32).ap()
        q_spill = nc.dram_tensor("q_spill", [P, HEADS, TOK], F32).ap()
        gate_spill = nc.dram_tensor("gate_spill", [P, 2 * KT, TOK], F32).ap()
        ga_spill = nc.dram_tensor("ga_spill", [P, HEADS, TOK], F32).ap()
        bias_spill = nc.dram_tensor("bias_spill", [NS, NKEY], F32).ap()

        with ExitStack() as area:
            x_rows = area.enter_context(nc.sbuf_tensor("x_rows", [P, 5, DM], F32))
            c_rows = area.enter_context(nc.sbuf_tensor("c_rows", [9, DM], F32))
        with ExitStack() as area:
            q_att = area.enter_context(nc.sbuf_tensor("q_att", [P, HEADS, TOK], F32))
            k_pages = area.enter_context(nc.sbuf_tensor("k_pages", [P, PAGES, KVW], F32))
            v_pages = area.enter_context(nc.sbuf_tensor("v_pages", [P, PAGES, KVW], F32))
            k_turned = area.enter_context(nc.sbuf_tensor("k_turned", [P, KVH, NKEY], F32))
            p_turned = area.enter_context(nc.sbuf_tensor("p_turned", [P, PAGES + 1, NS], F32))
            q_one = area.enter_context(nc.sbuf_tensor("q_one", [P, KVH, NS], F32))
        act_hi = sb("act_hi", [P, KT, TOK], F32R)
        act_lo = sb("act_lo", [P, KT, TOK], F32R)

        tab = sb("tab", [P, N_TAB])
        raw = sb("raw", [P, 4, 4, 256])
        w_hi_t = sb("w_hi_t", [P, 2, 4, 256], F32R)
        w_lo_t = sb("w_lo_t", [P, 2, 4, 256], F32R)
        x_t = sb("x_t", [P, KT * TOK])
        d_t = sb("d_t", [P, 8, TOK])
        stg = sb("stg", [P, 8 * TOK])
        k_new = sb("k_new", [P, KVH, TOK])
        ki_new = sb("ki_new", [P, TOK])
        wi_new = sb("wi_new", [IH, TOK])
        v_tok = sb("v_tok", [P, 5, KVW])
        k_tok = sb("k_tok", [P, 5, KVW])
        ki_tok = sb("ki_tok", [P, 5, ID])
        wi_tok = sb("wi_tok", [P, QT, IH])
        wi_mix = sb("wi_mix", [64, SEQS, NS])
        c_split = sb("c_split", [P, KT, 18], F32R)
        mod = sb("mod", [P, 48, 9])
        par_rows = sb("par_rows", [N_PAR, P])
        par = sb("par", [P, N_PAR])
        cw = sb("cw", [P, CT_, TAPS])
        pages = sb("pages", [1, SEQS * PAGES], I32)
        top8 = sb("top8", [P, 8])
        stat = sb("stat", [P, 16])
        eps = sb("eps", [P, 1])

        acc = ctx.enter_context(nc.psum_tensor("acc", [P, 4, 512], F32))
        aux = ctx.enter_context(nc.psum_tensor("aux", [P, 4, 512], F32))

        ident = tab[:, T_ID:T_ID + P]
        ones = tab[:, T_ONE:T_ONE + P]

        def pair(ap):
            return ap.rearrange("p (h n) -> p h n", h=2)

        def tabv(c):
            return pair(tab[:, c:c + TOK])

        def slot(i):
            return stg[:, i * TOK:(i + 1) * TOK]

        def samp(ap):
            return ap.rearrange("p (b t) -> p b t", t=STEPS)

        x_v = x_t[:, :].rearrange("p (k n) -> p k n", k=KT)
        X8 = 8 * TOK

        def xtile(k):
            return x_t[:, ds(k * TOK, TOK)] if not isinstance(k, int) else x_t[:, k * TOK:(k + 1) * TOK]

        NPR = P * (1 + 2 + 3 + 4)
        qoff = [0, P, 3 * P, 6 * P]
        work_p = x_t[:, 0:NPR]
        work_s = x_t[0:NS, NPR:NPR + NKEY]
        attn_o = x_v[:, 0:8, :]
        bias_p = x_t[:, X8:X8 + NPR]
        bias_s = x_t[0:NS, X8 + NPR:X8 + NPR + NKEY]
        state_rows = x_t[0:120, NPR + NKEY:NPR + NKEY + 512].rearrange("p (s h n) -> p s h n", s=2, h=2)
        tail2 = X8 + NPR + NKEY
        qi_all = x_t[:, tail2:tail2 + SEQS * 64].rearrange("p (b n) -> p b n", b=SEQS)
        u_tok = x_t[0:NS, tail2:tail2 + 512].rearrange("p (s h n) -> p s h n", s=2, h=2)
        p_tail = x_t[0:NS, tail2 + 512:tail2 + 512 + NS]
        conv_rows = stg[0:TAPS, 6 * TOK:6 * TOK + CW_]
        UB = SEQ + HIST
        UW = SEQS * (HIST + STEPS)
        u_pad = [stg[:, 4 * TOK + s * UB:4 * TOK + (s + 1) * UB] for s in range(2)]
        relu_p = stg[:, 0:2048].rearrange("p (s h n) -> p s h n", s=2, h=2)
        kx_pages = x_t[:, 0:2048].rearrange("p (s g n) -> p s g n", s=2, g=PAGES)
        kx_turned = stg[:, 2048:2560].rearrange("p (s n) -> p s n", s=2)
        relu_s = stg[0:64, 3072:4096].rearrange("p (s n) -> p s n", s=2)
        relu_tail = stg[0:64, 4096:4096 + NS]
        probs_p = stg[:, 0:4096].rearrange("p (s h n) -> p s h n", s=2, h=4)
        pt_p = k_turned[:, 0, 0:1024].rearrange("p (s n) -> p s n", s=2)
        probs_s = stg[0:NS, 0:NKEY]
        bias_rep = stg[0:NS, NKEY:2 * NKEY]

        raw_odd = d_t[:, :, :].rearrange("p k n -> p (k n)")[:, 0:4096].rearrange("p (i k n) -> p i k n", i=4, k=4)

        def ada_raw(i, odd):
            return raw_odd[:, i] if odd else raw[:, i]

        def ada_hi(i):
            return act_hi[:, 4 * i:4 * i + 4, 0:256]

        def ada_lo(i):
            return act_lo[:, 4 * i:4 * i + 4, 0:256]

        def accv(m):
            return acc[:, 2 * m:2 * m + 2, 0:HALF]

        names = """passed w_landed0 w_landed1 w_landed2 w_landed3 odd_landed0 odd_landed1 odd_landed2 odd_landed3 w_hi
            w_lo w_used acc0_ready acc0_free acc1_free params_in params_turned params_done state_copied
            row_ready mod_turned mod_done sq_ready xsum ssq_x rstd_x h_ready h_hi h_lo aux_ready swap_used
            std_ready rope_done tok_turned tok_done tok_stored q_spilled dots_ready relu_done score_done
            kx_landed0 kx_landed1 kx_turned_ps kx_copied sdots_ready srelu_done mixed score_s_done diag_done
            state_in0 state_in1 state_turned state_used u_done u_turned u_copied u_stored0 u_stored1 mean_in
            mean_ps mean_done cent_done csq_done cvar_in var_ps cstd_done ln_done silu_done act_stored0
            act_stored1 gc_done bias_done bias_stored q_back q_back_rest logits_p probs_raw ppeak_done exp_p
            p_ready ptr_p ptc_p pv_p ao_p k_landed k_turn_a k_turn_b k_cp_a k_cp_b q_one_done logits_s brep_in
            sraw_done exp_s ps_ready pts_ps pts_done pv_s ao_s ga_in0 ga_in1 ga_in2 ga_in3 ag_ready split_hi
            split_lo gates_in0 gates_in1 gates_used merged_hi merged_lo x_old_in0 x_old_in1 x_new_done dve
            arrived""".split()
        sems = {n: ctx.enter_context(nc.semaphore(n)) for n in names}
        layer_sems = range(sems["passed"].num, sems["arrived"].num + 1)
        assert len(layer_sems) == len(names)
        S = type("Sems", (), sems)
        w_landed = [S.w_landed0, S.w_landed1, S.w_landed2, S.w_landed3]
        odd_landed = [S.odd_landed0, S.odd_landed1, S.odd_landed2, S.odd_landed3]
        acc_free = [S.acc0_free, S.acc1_free]
        kx_landed, state_in, u_stored = [S.kx_landed0, S.kx_landed1], [S.state_in0, S.state_in1], [S.u_stored0, S.u_stored1]
        act_stored, gates_in, x_old_in = [S.act_stored0, S.act_stored1], [S.gates_in0, S.gates_in1], [S.x_old_in0, S.x_old_in1]
        ga_in = [S.ga_in0, S.ga_in1, S.ga_in2, S.ga_in3]
        layer_go = ctx.enter_context(nc.semaphore("layer_go"))
        tables_in = ctx.enter_context(nc.semaphore("tables_in"))
        rows_in = ctx.enter_context(nc.semaphore("rows_in"))
        pro_turned = ctx.enter_context(nc.semaphore("pro_turned"))
        pro_copied = ctx.enter_context(nc.semaphore("pro_copied"))
        pro_c = ctx.enter_context(nc.semaphore("pro_c"))
        v_landed = ctx.enter_context(nc.semaphore("v_landed"))
        x_kept = ctx.enter_context(nc.semaphore("x_kept"))
        eps_set = ctx.enter_context(nc.semaphore("eps_set"))
        y_turned = ctx.enter_context(nc.semaphore("y_turned"))
        y_copied = ctx.enter_context(nc.semaphore("y_copied"))
        y_stored = ctx.enter_context(nc.semaphore("y_stored"))
        block = ctx.enter_context(nc.Block())

        def hold(e, s, value):
            e.wait_ge(s, value)
            if not isinstance(value, int):
                e.sem_inc(S.passed, 1)

        class Steps:

            def __init__(self, e, s):
                self.e, self.s, self.n = e, s, 0

            def then(self, ins):
                ins.then_inc(self.s, 1)
                self.n += 1

            def wait(self, back=0):
                self.e.wait_ge(self.s, self.n - back)

            def close(self):
                self.wait()
                self.e.sem_clear(self.s)
                self.n = 0

        def end_of_layer(e, turn, clears=False):
            e.drain().then_inc(S.arrived, 1)
            if clears:
                e.wait_ge(S.arrived, 5)
                e.sem_clear(layer_sems)
                e.sem_inc(layer_go, 1)
            else:
                hold(e, layer_go, turn)

        def load_pages(e, dst, cache, b, landed):
            for g0 in range(0, PAGES, 8):
                numbers = [e.value_load(pages[0:1, ds(b * PAGES + (g0 + g), 1)], min_val=0, max_val=n_phys - 1) for g in range(8)]
                for g, page in enumerate(numbers):
                    e.dma_start(dst[:, g0 + g, :], cache[:, ds(page, 1)]).then_inc(landed, 16)

        TT = [(0, P), (P, P), (2 * P, P), (3 * P, P), (SEQ, NS)]

        @block.sync
        def _(sp):
            sp.dma_start(tab[:, :], table).then_inc(tables_in, 16)
            sp.dma_start(pages[:, :], page_table.rearrange("(a b) n -> a (b n)", a=1)).then_inc(tables_in, 16)
            sp.dma_start(c_rows[0:1, :], c_prompt).then_inc(rows_in, 16)
            sp.dma_start(c_rows[1:9, :], c_sample).then_inc(rows_in, 16)
            sp.dma_start(x_rows[:, 0:4, :], x_prompt.rearrange("a (t p) n -> p (a t) n", p=P)).then_inc(rows_in, 16)
            sp.dma_start(x_rows[0:NS, 4, :], x_sample.rearrange("b t n -> (b t) n")).then_inc(rows_in, 16)
            sp.wait_ge(pro_copied, 2 * KT)
            sp.dma_start(x_spill, x_v).then_inc(x_kept, 16)
            sp.wait_ge(tables_in, 32)
            end_of_layer(sp, 1, clears=True)

            def load(i, g, pieces):
                hold(sp, S.w_lo, 4 * g + i + 1)
                for dst, src, inc in pieces:
                    sp.dma_start(dst, src.rearrange("a (t p) n -> p (a t) n", p=P)).then_inc(w_landed[i], inc)

            with sp.Fori(0, DEPTH) as l:
                sp.sem_inc(S.w_lo, 4)
                one = ds(l, 1)

                def load_ada(g, odd, first=False):
                    for i in range(4):
                        if not first:
                            hold(sp, S.w_lo, 4 * g + (i - 3))
                        place, landed, inc = (ada_raw(i, odd), odd_landed[i], 48) if odd else (ada_raw(i, odd), w_landed[i], 96)
                        sp.dma_start(place, w_ada[one, 512 * i:512 * i + 512, ds(g * 256, 256)].rearrange(
                            "a (t p) n -> p (a t) n", p=P)).then_inc(landed, inc)

                load_ada(0, False, first=True)
                for r0, n, src in ((R_NORM, 16, norm_g), (R_BADA, 48, b_ada), (R_QG, 1, q_norm_g), (R_KG, 1, k_norm_g),
                                   (R_CB, 8, conv_b), (R_LG, 8, conv_ln_g), (R_LB, 8, conv_ln_b)):
                    sp.dma_start(par_rows[r0:r0 + n, :], src[one, :].rearrange("a (r p) -> (a r) p", p=P)).then_inc(S.params_in, 16)
                for a in range(2):
                    sp.dma_start(par_rows[R_IG:R_IG + 1, 64 * a:64 * a + 64], idx_k_norm_g[one, :]).then_inc(S.params_in, 16)
                sp.dma_start(conv_rows, conv_w[one].rearrange("a k c -> (a k) c")).then_inc(S.params_in, 16)
                sp.dma_start(cv_sample[one, :, 0:HIST - STEPS, :].rearrange("a b k c -> (a b) k c"),
                             state_conv[one, :, STEPS:HIST, :].rearrange("a b k c -> (a b) k c")).then_inc(S.state_copied, 16)
                load_ada(1, True, first=True)
                with sp.Fori(1, 12) as cc:
                    load_ada(cc * 2, False)
                    load_ada(cc * 2 + 1, True)

                def load_in(g0, n, col):
                    with sp.Fori(0, n) as c:
                        for i in range(4):
                            load(i, g0 + c, [(raw[:, i], w_in[one, 512 * i:512 * i + 512, ds(c * 256 + col, 256)], 48)])

                load_in(G_Q, 10, C_Q)
                for i in range(4):
                    rows = slice(512 * i, 512 * i + 512)
                    load(i, G_KI, [(raw[:, i, :, 0:64], w_in[one, rows, C_KI:C_KI + ID], 16),
                                   (raw[:, i, :, 64:128], w_in[one, rows, C_KI:C_KI + ID], 16),
                                   (raw[:, i, :, 128:256], w_in[one, rows, C_WI:C_WI + P], 16)])

                def load_glu(c):
                    for i in range(4):
                        rows = slice(512 * i, 512 * i + 512)
                        load(i, G_GLU + c, [(raw[:, i, :, 0:128], w_in[one, rows, ds(c * P + C_GLU, P)], 16),
                                            (raw[:, i, :, 128:256], w_in[one, rows, ds(c * P + (C_GLU + CW_), P)], 32)])

                load_glu(0)
                sp.wait_ge(S.rope_done, 2 + 21)
                sp.dma_start(q_spill, x_v[:, 0:8, :]).then_inc(S.q_spilled, 16)
                sp.wait_ge(S.tok_done, 1)
                for dst, dsts, src in ((k_prompt, k_sample, k_tok), (v_prompt, v_sample, v_tok)):
                    sp.dma_start(dst[one].rearrange("a b (t p) h d -> p (a b t) (h d)", p=P), src[:, 0:4, :]).then_inc(S.tok_stored, 16)
                    sp.dma_start(dsts[one].rearrange("a b t h d -> (a b t) (h d)"), src[0:NS, 4, :]).then_inc(S.tok_stored, 16)
                sp.dma_start(ki_prompt[one].rearrange("a b (t p) d -> p (a b t) d", p=P), ki_tok[:, 0:4, :]).then_inc(S.tok_stored, 16)
                sp.dma_start(ki_sample[one].rearrange("a b t d -> (a b t) d"), ki_tok[0:NS, 4, :]).then_inc(S.tok_stored, 16)
                sp.wait_ge(S.q_spilled, 16)
                for b in range(SEQS):
                    if b >= 2:
                        sp.wait_ge(S.kx_turned_ps, 4 * (b - 1))
                    load_pages(sp, kx_pages[:, b % 2], cache_kidx[one], b, kx_landed[b % 2])
                def load_state(c, s):
                    hold(sp, S.state_used, c + 1)
                    sp.dma_start(state_rows[:, s], state_conv[one].rearrange("a b k c -> (a b k) c")[:, ds(c * P, P)].rearrange(
                        "(h r) c -> r h c", h=2)).then_inc(state_in[s], 16)

                sp.wait_ge(S.q_spilled, 16)
                with sp.Fori(0, 3) as cc:
                    for s in range(2):
                        load_state(cc * 2 + s, s)
                        load_glu(cc * 2 + (s + 1))
                load_state(6, 0)
                load_glu(7)
                load_state(7, 1)
                load_in(G_MERGE, 16, C_MG)
                load_in(G_GA, 4, C_GA)
                load_in(G_GC, 4, C_GC)

                def load_branches(c):
                    for i in range(4):
                        w = w_conv_out if i < 2 else w_attn_out
                        load(i, G_MG + c, [(raw[:, i], w[one, 512 * (i % 2):512 * (i % 2) + 512, ds(c * 256, 256)], 48)])

                load_branches(0)
                sp.wait_ge(S.w_used, 4 * G_MG + 2)
                sp.dma_start(q_att[:, :, 0:P], q_spill[:, :, 0:P]).then_inc(S.q_back, 16)
                sp.dma_start(q_att[:, :, P:TOK], q_spill[:, :, P:TOK]).then_inc(S.q_back_rest, 16)
                sp.wait_ge(S.bias_done, 1)
                sp.dma_start(bias_spill, bias_s).then_inc(S.bias_stored, 16)
                rows_k = cache_k.rearrange("l g p h d -> l g p (h d)")[one]

                def load_k(b):
                    hold(sp, S.k_turn_a, 4 * b + 4)
                    hold(sp, S.k_turn_b, 4 * b + 4)
                    load_pages(sp, k_pages, rows_k, b, S.k_landed)

                def load_bias(b):
                    hold(sp, S.sraw_done, b + 1)
                    for r in range(HEADS):
                        sp.dma_start(bias_rep[STEPS * r:STEPS * r + STEPS, :], bias_spill[ds(b * STEPS, STEPS), :]).then_inc(S.brep_in, 16)

                sp.wait_ge(S.bias_stored, 16)
                load_k(0)
                sp.wait_ge(S.ao_p, 8)
                load_bias(0)
                with sp.Fori(0, SEQS - 1) as b:
                    load_k(b + 1)
                    load_bias(b + 1)
                sp.wait_ge(S.ao_s, 8)
                for h in range(HEADS):
                    if h >= 4:
                        sp.wait_ge(S.ag_ready, h - 3)
                    sp.dma_start(slot(h % 4), ga_spill[:, h, :]).then_inc(ga_in[h % 4], 16)
                def load_gates(c, s):
                    sp.wait_ge(S.split_lo, 16)
                    hold(sp, S.gates_used, c + 1)
                    for a in range(2):
                        sp.dma_start(stg[:, (4 * s + 2 * a) * TOK:(4 * s + 2 * a + 2) * TOK].rearrange("p (k n) -> p k n", k=2),
                                     gate_spill[:, ds(c * 2 + (1 - a) * KT, 2), :]).then_inc(gates_in[s], 16)

                with sp.Fori(0, 3) as cc:
                    for s in range(2):
                        load_gates(cc * 2 + s, s)
                        load_branches(cc * 2 + (s + 1))
                load_gates(6, 0)
                load_branches(7)
                load_gates(7, 1)
                hold(sp, x_kept, l * 16 + 16)
                with sp.Fori(0, 4) as cc:
                    for s in range(2):
                        c = cc * 2 + s
                        for i in range(4):
                            load(i, G_OUT + c, [(raw[:, i], w_out[one, 512 * i:512 * i + 512, ds(c * 256, 256)], 48)])
                        sp.wait_ge(S.gates_used, 2 + 8)
                        hold(sp, S.x_new_done, c * 2 + 2)
                        sp.dma_start(stg[:, 2 * s * TOK:(2 * s + 2) * TOK].rearrange("p (k n) -> p k n", k=2),
                                     x_spill[:, ds(c * 2, 2), :]).then_inc(x_old_in[s], 16)
                sp.wait_ge(S.x_new_done, 4 + KT)
                sp.dma_start(x_spill, x_v).then_inc(x_kept, 16)
                sp.wait_ge(S.tok_stored, 16 * 6)
                sp.wait_ge(S.state_copied, 16)
                end_of_layer(sp, None, clears=True)
            for t, (t0, n) in enumerate(TT):
                sp.wait_ge(y_copied, 4 * (t + 1))
                dst = y_prompt[0, t0:t0 + n, :] if t < 4 else y_sample.rearrange("b t n -> (b t) n")
                sp.dma_start(dst, x_rows[0:n, t, :]).then_inc(y_stored, 16)
            sp.wait_ge(y_stored, 16 * 5)
            sp.wait_ge(x_kept, 16 * (DEPTH + 1))

        @block.gpsimd
        def _(pool):
            end_of_layer(pool, 1)

            def lo(i, g):
                hold(pool, S.w_hi, 4 * g + i + 1)
                pool.tensor_tensor(w_lo_t[:, i % 2], raw[:, i], w_hi_t[:, i % 2].bitcast(F32), ALU.subtract).then_inc(S.w_lo, 1)

            def groups(g0, n):
                with pool.Fori(0, n) as c:
                    lo(2, g0 + c)
                    lo(3, g0 + c)
                    lo(0, g0 + c + 1)
                    lo(1, g0 + c + 1)

            with pool.Fori(0, DEPTH) as l:
                pool.sem_inc(S.h_lo, 2)
                with pool.Fori(0, KT // 2) as kk:
                    for s in range(2):
                        kt = kk * 2 + s
                        hold(pool, S.h_hi, kt + 1)
                        pool.tensor_tensor(act_lo[:, ds(kt, 1), :].rearrange("p a n -> p (a n)"), slot(4 + s),
                                           act_hi[:, ds(kt, 1), :].rearrange("p a n -> p (a n)").bitcast(F32), ALU.subtract).then_inc(S.h_lo, 1)
                pool.wait_ge(S.w_lo, 4 + 4 * G_IN + 2)
                groups(G_IN, 43)
                pool.wait_ge(S.ao_p, 8)
                rows_v = cache_v.rearrange("l g p h d -> l g p (h d)")[ds(l, 1)]
                with pool.Fori(0, SEQS) as b:
                    hold(pool, S.pv_s, b + 1)
                    load_pages(pool, v_pages, rows_v, b, v_landed)
                groups(G_MG, 8)
                groups(G_OUT, 7)
                lo(2, N_GROUPS - 1)
                lo(3, N_GROUPS - 1)
                end_of_layer(pool, l + 2)

        @block.scalar
        def _(act):
            act.wait_ge(eps_set, 1)
            for k in range(KT):
                act.wait_ge(pro_turned, k + 1)
                act.activation(x_v[:, k, 0:SEQ], acc[:, 2 * (k % 2), :], ACT.Copy).then_inc(pro_copied, 1)
                act.activation(x_v[:, k, SEQ:TOK], acc[:, 2 * (k % 2) + 1, 0:NS], ACT.Copy).then_inc(pro_copied, 1)
            act.wait_ge(pro_turned, KT + 1)
            act.activation(slot(0)[:, 0:144], aux[:, 0, 0:144], ACT.Silu).then_inc(pro_c, 1)
            act.wait_ge(pro_c, 1)
            act.activation(c_split[:, :, 0:9], slot(0)[:, 0:144].rearrange("p (k n) -> p k n", n=9), ACT.Copy).then_inc(pro_c, 1)
            end_of_layer(act, 1)

            def hi(i, g):
                hold(act, w_landed[i], 48 * g + 48)
                hold(act, S.w_used, 4 * g + i + 1)
                act.activation(w_hi_t[:, i % 2], raw[:, i], ACT.Copy).then_inc(S.w_hi, 1)

            def split_ada(i, g, cc, odd, first=False):
                hold(act, odd_landed[i] if odd else w_landed[i], cc * 48 + 48 if odd else cc * 96 + 96)
                if not first:
                    hold(act, S.w_used, 4 * g + (i - 1))
                act.activation(ada_hi(i), ada_raw(i, odd), ACT.Copy).then_inc(S.w_hi, 1)

            with act.Fori(0, DEPTH) as l:
                for i in range(4):
                    split_ada(i, 0, 0, False, first=True)
                def copy_rows(g, s):
                    hold(act, S.w_used, 4 * g + 6)
                    hold(act, S.mod_turned, g + 1)
                    act.activation(slot(7)[0:18, 256 * s:256 * s + 256], acc[0:18, 2 * s, 0:256], ACT.Copy).then_inc(S.row_ready, 1)

                def modulation(cc, with_x):
                    for s in range(2):
                        g = cc * 2 + s
                        for i in range(4):
                            split_ada(i, g + 1, cc + s, s == 0)
                        copy_rows(g, s)
                        if with_x:
                            hold(act, S.xsum, g + 1)
                            act.activation(slot(s), xtile(g), ACT.Square).then_inc(S.sq_ready, 1)

                with act.Fori(0, KT // 2) as cc:
                    modulation(cc, True)
                with act.Fori(KT // 2, 10) as cc:
                    modulation(cc, False)
                act.wait_ge(S.ssq_x, 1)
                act.activation(pair(slot(3)), aux[:, 0:2, 0:HALF], ACT.Sqrt, scale=1.0 / DM, bias=eps[:, :]).then_inc(S.rstd_x, 1)
                with act.Fori(10, 11) as cc:
                    modulation(cc, False)
                for i in range(4):
                    split_ada(i, 23, 11, True)
                copy_rows(22, 0)
                hi(0, G_IN)
                hi(1, G_IN)
                copy_rows(23, 1)
                with act.Fori(0, KT // 2) as kk:
                    for s in range(2):
                        kt = kk * 2 + s
                        hold(act, S.h_ready, kt + 1)
                        act.activation(act_hi[:, ds(kt, 1), :].rearrange("p a n -> p (a n)"), slot(4 + s), ACT.Copy).then_inc(S.h_hi, 1)

                def ready(m, g, a0):
                    if m == 0:
                        hold(act, S.acc0_ready, a0 + 1)
                    else:
                        hold(act, S.w_used, 4 * g + 6)

                def project1(g, t, gains, squares, aux_n, std_n, n_dim):
                    hi(2, g)
                    hi(3, g)
                    hi(0, g + 1)
                    for m in range(2):
                        if m == 1:
                            hi(1, g + 1)
                        ready(m, g, g - G_IN)
                        if gains[m] == "wi":
                            act.activation(pair(wi_new[:, :]), acc[0:IH, 2:4, 0:HALF], ACT.Copy,
                                           scale=IH ** -0.5 * ID ** -0.5).then_inc(acc_free[m], 1)
                            continue
                        hold(act, S.rope_done, t + m + 1)
                        gain = gains[m]
                        one_op = act.activation(pair(slot(m)), accv(m), ACT.Copy, scale=1.0 if gain is None else par[:, gain:gain + 1])
                        if squares:
                            one_op = act.activation(pair(slot(2 + m)), accv(m), ACT.Square)
                        one_op.then_inc(acc_free[m], 1)
                    if squares:
                        for m in range(squares):
                            hold(act, S.aux_ready, aux_n + m + 1)
                            act.activation(pair(slot(4 + m)), aux[:, 0:2, 0:HALF], ACT.Sqrt, scale=1.0 / n_dim,
                                           bias=eps[:, :]).then_inc(S.std_ready, 1)

                with act.Fori(0, 4) as c:
                    project1(G_Q + c, c * 2, (R_QG, R_QG), 2, c * 2, c * 2, HD)
                project1(G_K, 8, (R_KG, R_KG), 2, 8, 8, HD)
                project1(G_V, 10, (None, None), 0, 10, 10, HD)
                with act.Fori(0, 4) as c:
                    project1(G_QI + c, c * 2 + 12, (None, None), 0, 0, 0, ID)
                project1(G_KI, 20, (R_IG, "wi"), 1, 20, 10, ID)

                for u in range(4 * 8):
                    n = P * (u // 8 + 1)
                    act.wait_ge(S.dots_ready, u + 1)
                    if u >= 2:
                        act.wait_ge(S.score_done, u - 1)
                    act.activation(relu_p[:, u % 2, :, 0:n], aux[:, 2 * (u % 2):2 * (u % 2) + 2, 0:n], ACT.Relu).then_inc(S.relu_done, 1)
                for f in range(4 * SEQS):
                    act.wait_ge(S.kx_turned_ps, f + 1)
                    if f >= 2:
                        act.wait_ge(S.sdots_ready, f - 1)
                    act.activation(kx_turned[:, f % 2, :], aux[:, 0, 0:256], ACT.Copy).then_inc(S.kx_copied, 1)

                for s in range(2):
                    act.sem_inc(u_stored[s], 32)
                    act.sem_inc(act_stored[s], 16)
                act.sem_inc(S.u_copied, 1)

                def glu(c, s):
                    g = G_GLU + c
                    hi(2, g)
                    hi(3, g)
                    hi(0, g + 1)
                    ready(0, g, g - G_IN)
                    hold(act, S.u_done, c + 1)
                    act.activation(pair(slot(s)), accv(0), ACT.Copy).then_inc(acc_free[0], 1)
                    hi(1, g + 1)
                    ready(1, g, None)
                    act.activation(pair(slot(2 + s)), accv(1), ACT.Sigmoid).then_inc(acc_free[1], 1)

                def state_out(c, s, cc):
                    hold(act, S.u_turned, c + 1)
                    hold(act, u_stored[s], cc * 32 + 32)
                    act.activation(u_tok[:, s], aux[0:NS, 1, 0:256].rearrange("p (h n) -> p h n", h=2), ACT.Copy).then_inc(S.u_copied, 1)
                    hold(act, S.u_copied, c + 2)
                    act.dma_start(cv_prompt[ds(l, 1), :, :, ds(c * P, P)].rearrange("a b k c -> (a b k) c"),
                                  u_tok[0:HIST, s, 0, :]).then_inc(u_stored[s], 16)
                    act.dma_start(cv_sample[ds(l, 1), :, HIST - STEPS:HIST, ds(c * P, P)].rearrange("a b k c -> (a b) k c"),
                                  u_tok[:, s, 1, :]).then_inc(u_stored[s], 16)

                glu(0, 0)
                with act.Fori(0, 3) as cc:
                    for s in range(2):
                        glu(cc * 2 + (s + 1), 1 - s)
                        state_out(cc * 2 + s, s, cc)
                glu(7, 1)
                state_out(6, 0, 3)
                state_out(7, 1, 3)
                act.wait_ge(S.u_done, 2 + 8)

                def gates(g0, n, n0, func, dst, tile0):
                    with act.Fori(0, n) as c:
                        g = g0 + c
                        hi(2, g)
                        hi(3, g)
                        hi(0, g + 1)
                        for m in range(2):
                            if m == 1:
                                hi(1, g + 1)
                            ready(m, g, g - G_IN)
                            hold(act, act_stored[m], c * 16 + (n0 // 2 + 1) * 16)
                            act.activation(pair(slot(m)), accv(m), func).then_inc(acc_free[m], 1)
                            hold(act, acc_free[m], g - G_IN + 2)
                            act.dma_start(dst[:, ds(c * 2 + (tile0 + m), 1), :].rearrange("p a n -> p (a n)"), slot(m)).then_inc(act_stored[m], 16)

                gates(G_MERGE, 8, 0, ACT.Sigmoid, gate_spill, 0)
                act.wait_ge(S.mean_ps, 1)
                act.activation(pair(slot(2)), aux[:, 0:2, 0:HALF], ACT.Copy, scale=1.0 / CW_).then_inc(S.mean_done, 1)

                def squares(js):
                    for j in js:
                        act.wait_ge(S.cent_done, j + 1)
                        if j >= 2:
                            act.wait_ge(S.cvar_in, j - 1)
                        act.activation(slot(4 + j % 2), d_t[:, j, :], ACT.Square).then_inc(S.csq_done, 1)

                squares(range(0, 4))
                gates(G_MERGE + 8, 1, 16, ACT.Sigmoid, gate_spill, 16)
                squares(range(4, 8))
                gates(G_MERGE + 9, 4, 18, ACT.Sigmoid, gate_spill, 18)
                act.wait_ge(S.var_ps, 1)
                act.activation(pair(slot(3)), aux[:, 2:4, 0:HALF], ACT.Sqrt, scale=1.0 / CW_, bias=eps[:, :]).then_inc(S.cstd_done, 1)

                def swish(js):
                    for j in js:
                        act.wait_ge(S.ln_done, j + 1)
                        act.activation(d_t[:, j, :], d_t[:, j, :], ACT.Silu, scale=par[:, R_LG + j:R_LG + j + 1],
                                       bias=par[:, R_LB + j:R_LB + j + 1]).then_inc(S.silu_done, 1)

                gates(G_MERGE + 13, 1, 26, ACT.Sigmoid, gate_spill, 26)
                swish(range(0, 4))
                gates(G_MERGE + 14, 1, 28, ACT.Sigmoid, gate_spill, 28)
                swish(range(4, 8))
                gates(G_MERGE + 15, 1, 30, ACT.Sigmoid, gate_spill, 30)
                gates(G_GA, 4, 32, ACT.Silu, ga_spill, 0)
                for m in range(2):
                    act.wait_ge(act_stored[m], 16 + 20 * 16)
                with act.Fori(0, 4) as c:
                    g = G_GC + c
                    hi(2, g)
                    hi(3, g)
                    hi(0, g + 1)
                    for m in range(2):
                        if m == 1:
                            hi(1, g + 1)
                        ready(m, g, g - G_IN)
                        hold(act, S.gc_done, c * 2 + (m + 1))
                        act.activation(pair(slot(m)), accv(m), ACT.Silu).then_inc(acc_free[m], 1)

                for u in range(8):
                    n = P * (u // 2 + 1)
                    act.wait_ge(S.ppeak_done, u + 1)
                    for h in range(4):
                        last = act.activation(probs_p[:, u % 2, h, 0:n], probs_p[:, u % 2, h, 0:n], ACT.Exp,
                                              bias=stat[:, 4 + h:5 + h], accum_out=stat[:, 8 + h:9 + h])
                    last.then_inc(S.exp_p, 1)
                    for k in range(u // 2 + 1):
                        f = sum(v // 2 + 1 for v in range(u)) + k
                        act.wait_ge(S.ptr_p, f + 1)
                        if f >= 2:
                            act.wait_ge(S.ptc_p, f - 1)
                        act.activation(pt_p[:, f % 2, :], aux[:, f % 2, :], ACT.Copy).then_inc(S.pv_p, 1)

                def k_copies(b, fs):
                    for f in fs:
                        hold(act, S.k_turn_a, b * 4 + (4 + f // 2 + 1))
                        act.activation(k_turned[:, f // 4, (f % 4) * 512:(f % 4) * 512 + 512], aux[:, 1, :], ACT.Copy).then_inc(S.k_cp_a, 1)

                def soft(b):
                    hold(act, S.sraw_done, b + 2)
                    act.activation(probs_s, probs_s, ACT.Exp, bias=stat[0:NS, 1:2], accum_out=stat[0:NS, 2:3]).then_inc(S.exp_s, 1)

                act.wait_ge(S.ptc_p, 20)
                k_copies(0, (0, 2, 4, 6))
                with act.Fori(0, SEQS - 1) as b:
                    k_copies(b + 1, (0, 2))
                    soft(b)
                    k_copies(b + 1, (4, 6))
                soft(SEQS - 1)

                for n in range(16):
                    if n < 8:
                        act.wait_ge(S.pv_s, 1 + 8)
                        act.activation(act_hi[:, n, :], d_t[:, n, :], ACT.Copy).then_inc(S.split_hi, 1)
                    else:
                        act.wait_ge(S.ag_ready, n - 7)
                        act.activation(act_lo[:, n - 8, :], slot(4 + n % 4), ACT.Copy).then_inc(S.split_hi, 1)

                def only_splits(g0, n):
                    with act.Fori(0, n) as c:
                        hi(2, g0 + c)
                        hi(3, g0 + c)
                        hi(0, g0 + c + 1)
                        hi(1, g0 + c + 1)

                only_splits(G_MG, 8)
                for k in range(KT):
                    act.wait_ge(S.gates_used, 2 + 8)
                    act.activation(act_hi[:, k, :], xtile(k), ACT.Copy).then_inc(S.merged_hi, 1)
                only_splits(G_OUT, 7)
                hi(2, N_GROUPS - 1)
                hi(3, N_GROUPS - 1)
                for s in range(2):
                    act.wait_ge(u_stored[s], 32 + 32 * 4)
                end_of_layer(act, l + 2)
            for t, (t0, n) in enumerate(TT):
                for f in range(4):
                    i = 4 * t + f
                    act.wait_ge(y_turned, i + 1)
                    act.activation(x_rows[0:n, t, 512 * f:512 * f + 512], acc[0:n, i % 4, :], ACT.Copy).then_inc(y_copied, 1)

        @block.tensor
        def _(pe):
            pe.wait_ge(tables_in, 32)
            pe.wait_ge(rows_in, 64)
            for k in range(KT):
                if k >= 2:
                    pe.wait_ge(pro_copied, 2 * (k - 1))
                for t, (t0, n) in enumerate(TT):
                    out = acc[:, 2 * (k % 2), t0:t0 + n] if t < 4 else acc[:, 2 * (k % 2) + 1, 0:n]
                    last = pe.transpose(out, x_rows[0:n, t, k * P:(k + 1) * P], ident[0:n, 0:n])
                last.then_inc(pro_turned, 1)
            for k in range(KT):
                last = pe.transpose(aux[:, 0, 9 * k:9 * k + 9], c_rows[:, k * P:(k + 1) * P], ident[0:9, 0:9])
            last.then_inc(pro_turned, 1)
            end_of_layer(pe, 1)

            def group(g, sets, rhs=None, before=None):
                for b0, b1, a0, a1 in sets:
                    for i in range(b0, b1 + 1):
                        hold(pe, S.w_lo, 4 * g + i + 5)
                        if before:
                            pe.wait_ge(before[0], before[1] + 4 * (i + 1))
                        for m in range(2):
                            if i == b0:
                                hold(pe, acc_free[m], (a0, a1)[m] + 1)
                            for k in range(4):
                                kt = 4 * (i - b0) + k
                                hi_r, lo_r = rhs(i, kt)
                                for n, (w, x) in enumerate(((w_hi_t, hi_r), (w_hi_t, lo_r), (w_lo_t, hi_r))):
                                    for h in range(2):
                                        last = pe.matmul(acc[:, 2 * m + h, 0:HALF], w[:, i % 2, k, P * m:P * m + P],
                                                         x[:, h * HALF:(h + 1) * HALF],
                                                         start=i == b0 and k == 0 and n == 0, stop=i == b1 and k == 3 and n == 2)
                            if i == b1 and m == 0:
                                last.then_inc(S.acc0_ready, 1)
                        last.then_inc(S.w_used, 1)

            def of_h(i, kt):
                return act_hi[:, kt, :], act_lo[:, kt, :]

            def fp32_pair(bank, lhsT, rhs):
                for h in range(2):
                    last = pe.matmul(aux[:, bank + h, 0:HALF], lhsT, rhs[:, h * HALF:(h + 1) * HALF], start=True, stop=True)
                return last

            with pe.Fori(0, DEPTH) as l:
                pe.sem_inc(S.w_used, 2)
                pe.sem_inc(S.acc0_free, 1)
                pe.sem_inc(S.acc1_free, 1)
                pe.sem_inc(S.mod_turned, 2)
                pe.sem_inc(S.k_turn_a, 4)
                pe.sem_inc(S.k_turn_b, 4)
                pe.sem_inc(S.pv_s, 1)
                pe.wait_ge(S.params_in, 160)
                pe.transpose(aux[:, 2, 0:N_PAR], par_rows[:, :], ident[0:N_PAR, 0:N_PAR])
                for j in range(CT_):
                    last = pe.transpose(aux[:, 3, TAPS * j:TAPS * (j + 1)], conv_rows[:, j * P:(j + 1) * P], ident[0:TAPS, 0:TAPS])
                last.then_inc(S.params_turned, 1)
                pe.wait_ge(S.params_done, 1)

                def ada(g, s):
                    for i in range(4):
                        hold(pe, S.w_lo, 4 * g + (i + 5))
                        for k in range(4):
                            for n, w in enumerate((ada_hi(i), ada_lo(i))):
                                last = pe.matmul(acc[0:18, 2 * s, 0:256], c_split[:, 4 * i + k, :], w[:, k, :],
                                                 start=i == 0 and k == 0 and n == 0, stop=i == 3 and k == 3 and n == 1)
                        last.then_inc(S.w_used, 1)

                def turn_rows(g, s):
                    hold(pe, S.row_ready, g + 1)
                    hold(pe, S.mod_done, g + 1)
                    for a in range(2):
                        last = pe.matmul(aux[:, 2 + s, 9 * a:9 * a + 9], slot(7)[0:18, 256 * s + P * a:256 * s + P * a + P],
                                         tab[0:18, T_COMB:T_COMB + 9], start=True, stop=True)
                    last.then_inc(S.mod_turned, 1)

                def ada_pair(cc):
                    for s in range(2):
                        ada(cc * 2 + (s + 1), 1 - s)
                        turn_rows(cc * 2 + s, s)

                ada(0, 0)
                with pe.Fori(0, 9) as cc:
                    ada_pair(cc)
                pe.wait_ge(S.xsum, 2 + KT)
                fp32_pair(0, ones, slot(2)).then_inc(S.ssq_x, 1)
                with pe.Fori(9, 11) as cc:
                    ada_pair(cc)
                ada(23, 1)
                turn_rows(22, 0)
                turn_rows(23, 1)

                def part1(g, kinds, aux_n, js, jn, before=None):
                    a = g - G_IN
                    group(g, [(0, 3, a, a)], of_h, before)
                    for m, kind in enumerate(kinds):
                        if kind is None:
                            continue
                        hold(pe, acc_free[m], a + 2)
                        hold(pe, S.swap_used, js + m + 1)
                        if kind == "v":
                            for t, (t0, n) in enumerate(TT):
                                out = aux[:, 2, t0:t0 + n] if t < 4 else aux[0:n, 3, 0:P]
                                last = pe.transpose(out, slot(m)[:, t0:t0 + n], ident)
                        else:
                            sw = T_SWQ if kind == "q" else T_SWI
                            if kind != "qi":
                                hold(pe, S.std_ready, jn + m + 1)
                                fp32_pair(0, tab[:, T_ONE64:T_ONE64 + P] if kind == "ki" else ones, slot(2 + m))
                            last = fp32_pair(2, tab[:, sw:sw + P], slot(m))
                        last.then_inc(S.aux_ready, 1)

                part1(G_Q, ("q", "q"), 0, 0, 0, before=(S.h_lo, 2))
                with pe.Fori(1, 4) as c:
                    part1(G_Q + c, ("q", "q"), c * 2, c * 2, c * 2)
                part1(G_K, ("q", "q"), 8, 8, 8)
                part1(G_V, ("v", "v"), 10, 10, 10)
                with pe.Fori(0, 4) as c:
                    part1(G_QI + c, ("qi", "qi"), c * 2 + 12, c * 2 + 12, 10)
                part1(G_KI, ("ki", None), 20, 20, 10)

                pe.wait_ge(S.rope_done, 2 + 21)
                pe.wait_ge(S.acc1_free, 11 + 1)
                for t, (t0, n) in enumerate(TT):
                    main = t < 4
                    for h in range(KVH):
                        out = aux[:, h, t0:t0 + n] if main else aux[0:n, 3, P * h:P * h + P]
                        pe.transpose(out, k_new[:, h, t0:t0 + n], ident)
                    out = aux[:, 2, ID * t:ID * t + ID] if main else aux[0:n, 3, 256:256 + ID]
                    pe.transpose(out, ki_new[0:ID, t0:t0 + n], ident[0:ID, 0:ID])
                    if main:
                        pe.transpose(aux[:, 2, 256 + IH * t:256 + IH * t + IH], wi_new[:, t0:t0 + n], ident[0:IH, 0:IH])
                pe.matmul(aux[0:64, 3, 320:320 + NS], tab[0:IH, T_EXP:T_EXP + 64], wi_new[:, SEQ:TOK],
                          start=True, stop=True).then_inc(S.tok_turned, 1)

                pe.wait_ge(S.tok_done, 1)
                for u in range(4 * 8):
                    qt, j = divmod(u, 8)
                    n = P * (qt + 1)
                    if u >= 2:
                        pe.wait_ge(S.relu_done, u - 1)
                    for h in range(2):
                        last = pe.matmul(aux[:, 2 * (u % 2) + h, 0:n], d_t[64 * h:64 * h + 64, j, qt * P:qt * P + P],
                                         ki_new[64 * h:64 * h + 64, 0:n], start=True, stop=True)
                    last.then_inc(S.dots_ready, 1)

                pe.wait_ge(S.diag_done, 1)
                pe.wait_ge(S.relu_done, 32)
                pe.wait_ge(S.acc0_free, 1 + 11)

                def turn_x(f):
                    b, ch = divmod(f, 4)
                    pe.wait_ge(kx_landed[b % 2], 256 * (b // 2 + 1))
                    if f >= 1:
                        pe.wait_ge(S.kx_copied, f)
                    for g in range(2):
                        two_pages = kx_pages[:, b % 2, 4 * ch + 2 * g:4 * ch + 2 * g + 2, :].rearrange("p g n -> p (g n)")
                        last = pe.transpose(aux[:, 0, P * g:P * g + P], two_pages, ident)
                    last.then_inc(S.kx_turned_ps, 1)

                def dots_x(f):
                    pe.wait_ge(S.kx_copied, f + 1)
                    if f >= 1:
                        pe.wait_ge(S.srelu_done, f)
                    for h in range(2):
                        half = slice(64 * h, 64 * h + 64)
                        last = pe.matmul(aux[0:64, 2 + h, 0:256], qi_all[half, f // 4, :], kx_turned[half, f % 2, :], start=True, stop=True)
                    last.then_inc(S.sdots_ready, 1)

                def mix_x(f):
                    b, ch = divmod(f, 4)
                    pe.wait_ge(S.srelu_done, f + 1)
                    pe.matmul(acc[0:NS, ch, :], wi_mix[:, b, :], relu_s[:, f % 2, :], start=b == 0,
                              stop=b == SEQS - 1).then_inc(S.mixed, 1)

                NF = 4 * SEQS
                for f in range(NF + 2):
                    if f < NF:
                        turn_x(f)
                    if 1 <= f <= NF:
                        dots_x(f - 1)
                    if f >= 2:
                        mix_x(f - 2)
                pe.wait_ge(S.srelu_done, NF)
                for b in range(SEQS):
                    last = pe.matmul(aux[0:64, 2, STEPS * b:STEPS * b + STEPS], qi_all[0:64, b, :],
                                     ki_new[0:64, SEQ + STEPS * b:SEQ + STEPS * b + STEPS], start=True, stop=True)
                last.then_inc(S.sdots_ready, 1)
                pe.wait_ge(S.srelu_done, NF + 1)
                for b in range(SEQS):
                    last = pe.matmul(aux[0:NS, 1, 0:STEPS], wi_mix[:, b, :], relu_tail[:, STEPS * b:STEPS * b + STEPS],
                                     start=b == 0, stop=b == SEQS - 1)
                last.then_inc(S.mixed, 1)
                pe.wait_ge(S.score_s_done, 1)

                def glu(c, s, cc):
                    g = G_GLU + c
                    group(g, [(0, 3, g - G_IN, g - G_IN)], of_h)
                    hold(pe, state_in[s], cc * 16 + 16)
                    hold(pe, S.state_turned, c + 1)
                    for h in range(2):
                        last = pe.transpose(aux[:, 0, 120 * h:120 * h + 120], state_rows[:, s, h, :], ident[0:120, 0:120])
                    last.then_inc(S.state_used, 1)

                def turn_u(c, s):
                    hold(pe, S.u_done, c + 3)
                    hold(pe, S.u_copied, c + 1)
                    pe.transpose(aux[0:HIST, 1, 0:P], u_pad[s][:, SEQ:SEQ + HIST], ident)
                    pe.transpose(aux[0:NS, 1, P:2 * P], slot(s)[:, SEQ:TOK], ident).then_inc(S.u_turned, 1)

                glu(0, 0, 0)
                with pe.Fori(0, 3) as cc:
                    for s in range(2):
                        glu(cc * 2 + (s + 1), 1 - s, cc + s)
                        turn_u(cc * 2 + s, s)
                glu(7, 1, 3)
                turn_u(6, 0)
                turn_u(7, 1)

                def plain(g0, n):
                    with pe.Fori(0, n) as c:
                        group(g0 + c, [(0, 3, g0 + c - G_IN, g0 + c - G_IN)], of_h)

                plain(G_MERGE, 6)
                pe.wait_ge(S.mean_in, 1)
                fp32_pair(0, ones, slot(7)).then_inc(S.mean_ps, 1)
                plain(G_MERGE + 6, 7)
                pe.wait_ge(S.cvar_in, CT_)
                fp32_pair(2, ones, slot(6)).then_inc(S.var_ps, 1)
                plain(G_MERGE + 13, 11)

                pe.wait_ge(S.q_back, 16)
                pe.wait_ge(S.bias_done, 1)
                pe.wait_ge(S.acc0_free, 1 + 43)
                pe.wait_ge(S.acc1_free, 1 + 43)

                def logits(u):
                    qt, g = divmod(u, KVH)
                    n = P * (qt + 1)
                    if u == 2:
                        pe.wait_ge(S.q_back_rest, 16)
                    if u >= 1:
                        pe.wait_ge(S.probs_raw, u)
                    for h in range(GROUP):
                        last = pe.matmul(acc[:, h, 0:n], q_att[:, GROUP * g + h, qt * P:qt * P + P], k_new[:, g, 0:n], start=True, stop=True)
                    last.then_inc(S.logits_p, 1)

                def values(u):
                    qt, g = divmod(u, KVH)
                    f0 = sum(v // 2 + 1 for v in range(u))
                    pe.wait_ge(S.p_ready, u + 1)
                    if u >= 2:
                        pe.wait_ge(S.ao_p, u - 1)

                    def turn(k):
                        if f0 + k >= 2:
                            pe.wait_ge(S.pv_p, f0 + k - 1)
                        for h in range(GROUP):
                            last = pe.transpose(aux[:, (f0 + k) % 2, P * h:P * h + P], probs_p[:, u % 2, h, k * P:k * P + P], ident)
                        last.then_inc(S.ptr_p, 1)

                    turn(0)
                    for k in range(qt + 1):
                        if k < qt:
                            turn(k + 1)
                        pe.wait_ge(S.pv_p, f0 + k + 1)
                        pe.matmul(aux[:, 2 + u % 2, :], v_tok[:, k, g * HD:(g + 1) * HD], pt_p[:, (f0 + k) % 2, :],
                                  start=k == 0, stop=k == qt).then_inc(S.ptc_p, 1)

                logits(0)
                for u in range(8):
                    if u < 7:
                        logits(u + 1)
                    values(u)
                pe.wait_ge(S.ao_p, 8)

                def turn_k(b):
                    hold(pe, S.k_landed, b * 256 + 256)
                    for f in range(8):
                        bank, done, ready_ = (1, S.k_cp_a, S.k_turn_a) if f % 2 == 0 else (2, S.k_cp_b, S.k_turn_b)
                        if f >= 2:
                            hold(pe, done, b * 4 + (f // 2 + 1))
                        for g in range(4):
                            last = pe.transpose(aux[:, bank, P * g:P * g + P],
                                                k_pages[:, 4 * (f % 4) + g, (f // 4) * HD:(f // 4) * HD + HD], ident)
                        last.then_inc(ready_, 1)

                def sample_logits(b):
                    hold(pe, S.k_cp_a, b * 4 + 5)
                    hold(pe, S.k_cp_b, b * 4 + 5)
                    hold(pe, S.q_one_done, b + 1)
                    hold(pe, S.sraw_done, b + 1)
                    for ch in range(5):
                        for g in range(KVH):
                            n = 512 if ch < 4 else STEPS
                            out = acc[0:NS, ch, 0:n] if ch < 4 else aux[0:NS, 0, 0:n]
                            last = pe.matmul(out, q_one[:, g, :], k_turned[:, g, ch * 512:ch * 512 + n], start=g == 0, stop=g == 1)
                    last.then_inc(S.logits_s, 1)

                def sample_values(b):
                    hold(pe, S.ps_ready, b + 1)
                    for k in range(PAGES):
                        pe.transpose(aux[:, 1, NS * k:NS * k + NS], probs_s[:, k * P:k * P + P], ident[0:NS, 0:NS])
                    pe.transpose(aux[0:NS, 2, 0:NS], p_tail, ident[0:NS, 0:NS]).then_inc(S.pts_ps, 1)
                    hold(pe, v_landed, l * (16 * PAGES * SEQS) + (b * 256 + 256))
                    hold(pe, S.pts_done, b + 1)
                    for g in range(KVH):
                        for k in range(PAGES + 1):
                            v = v_pages[:, k, g * HD:(g + 1) * HD] if k < PAGES else v_tok[0:NS, 4, g * HD:(g + 1) * HD]
                            p = p_turned[:, k, 16 * g:16 * g + 16] if k < PAGES else p_turned[0:NS, k, 16 * g:16 * g + 16]
                            last = pe.matmul(aux[:, 3, 16 * g:16 * g + 16], v, p, start=k == 0, stop=k == PAGES)
                    last.then_inc(S.pv_s, 1)

                turn_k(0)
                with pe.Fori(0, SEQS - 1) as b:
                    sample_logits(b)
                    turn_k(b + 1)
                    hold(pe, S.k_cp_a, b * 4 + 9)
                    hold(pe, S.k_cp_b, b * 4 + 9)
                    sample_values(b)
                    hold(pe, S.pts_done, b + 1)
                sample_logits(SEQS - 1)
                sample_values(SEQS - 1)

                def branches(c, before=None):
                    group(G_MG + c, [(0, 1, c * 2 + 43, c * 2 + 43), (2, 3, c * 2 + 44, c * 2 + 44)],
                          lambda i, kt: (act_hi[:, kt, :], act_hi[:, 8 + kt, :]) if i < 2 else (act_lo[:, kt, :], act_lo[:, 8 + kt, :]), before)

                branches(0, (S.split_lo, 0))
                with pe.Fori(1, 8) as c:
                    branches(c)
                with pe.Fori(0, 8) as c:
                    group(G_OUT + c, [(0, 3, c + 59, c + 59)], of_h, before=(S.merged_lo, 0))
                end_of_layer(pe, l + 2)
            for t, (t0, n) in enumerate(TT):
                for f in range(4):
                    i = 4 * t + f
                    if i >= 4:
                        pe.wait_ge(y_copied, i - 3)
                    for k in range(4):
                        last = pe.transpose(acc[0:n, i % 4, P * k:P * k + P], x_v[:, 4 * f + k, t0:t0 + n], ident)
                    last.then_inc(y_turned, 1)

        @block.vector
        def _(dve):
            dve.memset(eps[:, :], EPS).then_inc(eps_set, 1)
            dve.wait_ge(pro_c, 2)
            dve.tensor_tensor(c_split[:, :, 9:18], slot(0)[:, 0:144].rearrange("p (k n) -> p k n", n=9),
                              c_split[:, :, 0:9].bitcast(F32), ALU.subtract).then_inc(pro_c, 1)
            dve.wait_ge(pro_c, 3)
            end_of_layer(dve, 1)
            st = Steps(dve, S.dve)

            def bc(ap, n):
                return ap.unsqueeze(2).to_broadcast([ap.shape[0], ap.shape[1], n])

            with dve.Fori(0, DEPTH) as l:
                dve.sem_inc(S.rope_done, 2)
                dve.sem_inc(S.swap_used, 1)
                dve.sem_inc(S.std_ready, 1)
                dve.sem_inc(S.mod_done, 2)
                dve.memset(slot(2), 0.0).then_inc(S.xsum, 2)
                dve.wait_ge(S.params_turned, 1)
                st.then(dve.tensor_copy(par[:, :], aux[:, 2, 0:N_PAR]))
                dve.tensor_copy(cw[:, :, :].rearrange("p j k -> p (j k)"), aux[:, 3, 0:CT_ * TAPS]).then_inc(S.params_done, 1)
                def rest_ada(g, odd):
                    for i in range(4):
                        hold(dve, S.w_hi, 4 * g + (i + 1))
                        dve.tensor_tensor(ada_lo(i), ada_raw(i, odd), ada_hi(i).bitcast(F32), ALU.subtract).then_inc(S.w_lo, 1)

                def mod_columns(g, s):
                    hold(dve, S.mod_turned, g + 3)
                    dve.tensor_tensor(mod[:, ds(g * 2, 2), :], aux[:, 2 + s, 0:18].rearrange("p (a n) -> p a n", n=9),
                                      bc(par[:, ds(g * 2 + R_BADA, 2)], 9), ALU.add).then_inc(S.mod_done, 1)

                def modulation(cc, with_x):
                    for s in range(2):
                        g = cc * 2 + s
                        rest_ada(g + 2, s == 1)
                        if with_x:
                            hold(dve, S.sq_ready, g + 1)
                            hold(dve, S.xsum, g + 2)
                            dve.tensor_tensor(slot(2), slot(2), slot(s), ALU.add).then_inc(S.xsum, 1)
                        mod_columns(g, s)

                st.close()
                rest_ada(0, False)
                rest_ada(1, True)
                with dve.Fori(0, KT // 2) as cc:
                    modulation(cc, True)
                with dve.Fori(KT // 2, 10) as cc:
                    modulation(cc, False)
                dve.wait_ge(S.rstd_x, 1)
                st.then(dve.reciprocal(slot(3), slot(3)))
                with dve.Fori(10, 11) as cc:
                    modulation(cc, False)
                for i in range(2):
                    dve.wait_ge(S.w_hi, 4 * G_IN + i + 1)
                    dve.tensor_tensor(w_lo_t[:, i], raw[:, i], w_hi_t[:, i].bitcast(F32), ALU.subtract).then_inc(S.w_lo, 1)
                mod_columns(22, 0)
                mod_columns(23, 1)
                dve.wait_ge(S.mod_done, 2 + 24)
                st.then(dve.scalar_tensor_tensor(out=mod[:, 16:32, :], in0=mod[:, 16:32, :], scalar=1.0,
                                                 in1=bc(par[:, R_NORM:R_NORM + KT], 9), op0=ALU.add, op1=ALU.mult))
                st.close()
                hold(dve, x_kept, l * 16 + 16)
                with dve.Fori(0, KT // 2) as kk:
                    for s in range(2):
                        st.then(dve.tensor_tensor(slot(s), xtile(kk * 2 + s), slot(3), ALU.mult))
                    for s in range(2):
                        kt = kk * 2 + s
                        gain, shift = mod[:, ds(kt + 16, 1), :].rearrange("p a n -> p (a n)"), mod[:, ds(kt, 1), :].rearrange("p a n -> p (a n)")
                        hold(dve, S.h_lo, kt + 1)
                        st.wait(back=1)
                        st.then(dve.tensor_tensor(samp(slot(4 + s)[:, SEQ:TOK]), samp(slot(s)[:, SEQ:TOK]), bc(gain[:, 1:9], STEPS), ALU.mult))
                        st.then(dve.tensor_scalar(slot(4 + s)[:, 0:SEQ], slot(s)[:, 0:SEQ], gain[:, 0:1], shift[:, 0:1], ALU.mult, ALU.add))
                        st.wait()
                        dve.tensor_tensor(samp(slot(4 + s)[:, SEQ:TOK]), samp(slot(4 + s)[:, SEQ:TOK]), bc(shift[:, 1:9], STEPS),
                                          ALU.add).then_inc(S.h_ready, 1)
                    st.close()

                def rope(m, aux_n, jn, cos, sin, out, rows=P):
                    hold(dve, S.aux_ready, aux_n + 1)
                    e = pair(slot(6 + m))
                    dve.tensor_tensor(e, aux[:, 2:4, 0:HALF], tabv(sin), ALU.mult).then_inc(S.swap_used, 1)
                    st.then(dve.tensor_tensor(slot(m), slot(m), tab[:, cos:cos + TOK], ALU.mult))
                    st.wait()
                    if jn is None:
                        dve.tensor_tensor(out, slot(6 + m), slot(m), ALU.add).then_inc(S.rope_done, 1)
                        st.close()
                        return
                    st.then(dve.tensor_tensor(slot(6 + m), slot(6 + m), slot(m), ALU.add))
                    hold(dve, S.std_ready, jn + 2)
                    st.then(dve.reciprocal(slot(4 + m), slot(4 + m)))
                    st.close()
                    dve.tensor_tensor(out, slot(6 + m), slot(4 + m), ALU.mult).then_inc(S.rope_done, 1)

                with dve.Fori(0, 4) as c:
                    for m in range(2):
                        rope(m, c * 2 + m, c * 2 + m, T_CQ, T_SQ, xtile(c * 2 + m))
                for m in range(2):
                    rope(m, 8 + m, 8 + m, T_CQ, T_SQ, k_new[:, m, :])
                for m in range(2):
                    dve.wait_ge(S.aux_ready, 11 + m)
                    dve.tensor_copy(v_tok[:, 0:4, m * HD:(m + 1) * HD], aux[:, 2, :].rearrange("p (t d) -> p t d", t=4)).then_inc(S.rope_done, 1)
                    dve.tensor_copy(v_tok[0:NS, 4, m * HD:(m + 1) * HD], aux[0:NS, 3, 0:P]).then_inc(S.swap_used, 1)
                with dve.Fori(0, 4) as c:
                    for m in range(2):
                        rope(m, c * 2 + (12 + m), None, T_CI, T_SI, d_t[:, ds(c * 2 + m, 1), :].rearrange("p a n -> p (a n)"))
                rope(0, 20, 10, T_CI, T_SI, ki_new[:, :])

                dve.wait_ge(S.tok_turned, 1)
                dve.wait_ge(S.swap_used, 1 + 21)
                for h in range(KVH):
                    st.then(dve.tensor_copy(k_tok[:, 0:4, h * HD:(h + 1) * HD], aux[:, h, :].rearrange("p (t d) -> p t d", t=4)))
                st.then(dve.tensor_copy(ki_tok[:, 0:4, :], aux[:, 2, 0:256].rearrange("p (t d) -> p t d", t=4)))
                st.then(dve.tensor_copy(wi_tok[:, :, :], aux[:, 2, 256:320].rearrange("p (t d) -> p t d", t=4)))
                st.then(dve.tensor_copy(k_tok[0:NS, 4, :], aux[0:NS, 3, 0:256]))
                st.then(dve.tensor_copy(ki_tok[0:NS, 4, :], aux[0:NS, 3, 256:320]))
                mixin = aux[0:64, 3, 320:320 + NS].unsqueeze(1).to_broadcast([64, SEQS, NS])
                dve.tensor_tensor(wi_mix[:, :, :], mixin, tab[0:64, T_MASK:T_MASK + SEQS * NS].rearrange("p (b n) -> p b n", b=SEQS),
                                  ALU.mult).then_inc(S.tok_done, 1)
                for half in range(2):
                    for h in range(2):
                        src = d_t[64 * h:64 * h + 64, :, SEQ:TOK].rearrange("p j (b t) -> p b j t", t=STEPS)
                        dst = qi_all[64 * half:64 * half + 64, :, 32 * h:32 * h + 32].rearrange("p b (j t) -> p b j t", t=STEPS)
                        last = dve.tensor_copy(dst, src)
                last.then_inc(S.diag_done, 1)

                for u in range(4 * 8):
                    qt, j = divmod(u, 8)
                    n = P * (qt + 1)
                    score = bias_p[:, qoff[qt]:qoff[qt] + n]
                    dve.wait_ge(S.relu_done, u + 1)
                    w = [wi_tok[:, qt, 2 * j + h:2 * j + h + 1] for h in range(2)]
                    if j == 0:
                        st.then(dve.tensor_scalar(score, relu_p[:, u % 2, 0, 0:n], w[0], None, ALU.mult))
                    else:
                        st.then(dve.scalar_tensor_tensor(out=score, in0=relu_p[:, u % 2, 0, 0:n], scalar=w[0], in1=score,
                                                         op0=ALU.mult, op1=ALU.add))
                    st.close()
                    dve.scalar_tensor_tensor(out=score, in0=relu_p[:, u % 2, 1, 0:n], scalar=w[1], in1=score,
                                             op0=ALU.mult, op1=ALU.add).then_inc(S.score_done, 1)
                    dve.wait_ge(S.score_done, u + 1)
                    if j == 7:
                        d = score[:, qt * P:qt * P + P]
                        st.then(dve.tensor_tensor(d, d, tab[:, T_TRI:T_TRI + P], ALU.min))
                st.close()
                for f in range(4 * SEQS):
                    dve.wait_ge(S.sdots_ready, f + 1)
                    if f >= 2:
                        dve.wait_ge(S.mixed, f - 1)
                    dve.tensor_scalar(relu_s[:, f % 2, :].rearrange("p (g h n) -> p h g n", g=2, h=2),
                                      aux[0:64, 2:4, 0:256].rearrange("p h (g n) -> p h g n", g=2), 0.0, None, ALU.max).then_inc(S.srelu_done, 1)
                dve.wait_ge(S.sdots_ready, 4 * SEQS + 1)
                dve.tensor_scalar(relu_tail, aux[0:64, 2, 0:NS], 0.0, None, ALU.max).then_inc(S.srelu_done, 1)
                dve.wait_ge(S.mixed, 4 * SEQS + 1)
                st.then(dve.tensor_copy(bias_s[:, 0:PAST].rearrange("p (c n) -> p c n", c=4), acc[0:NS, :, :]))
                dve.tensor_tensor(bias_s[:, PAST:NKEY], aux[0:NS, 1, 0:STEPS], tab[0:NS, T_UMS:T_UMS + STEPS], ALU.min).then_inc(S.score_s_done, 1)
                dve.wait_ge(S.score_s_done, 1)
                st.close()

                dve.sem_inc(S.u_done, 2)
                dve.sem_inc(S.state_turned, 1)
                dve.sem_inc(S.state_used, 2)
                dve.sem_inc(S.gc_done, 2)
                for s in range(2):
                    st.then(dve.memset(u_pad[s][:, 0:HIST], 0.0))
                st.close()
                def make_u(c, s):
                    u = u_pad[s]
                    us = x_t[:, ds(c * UW, UW)].rearrange("p (b k) -> p b k", b=SEQS)
                    hold(dve, S.state_used, c + 3)
                    dve.tensor_copy(us[:, :, 0:HIST], aux[:, 0, 0:240].rearrange("p (b k) -> p b k", b=SEQS)).then_inc(S.state_turned, 1)
                    hold(dve, S.state_turned, c + 2)
                    a0 = G_GLU - G_IN
                    hold(dve, S.acc0_free, c + (a0 + 2))
                    hold(dve, S.acc1_free, c + (a0 + 2))
                    st.then(dve.tensor_tensor(u[:, HIST:HIST + SEQ], slot(s)[:, 0:SEQ], slot(2 + s)[:, 0:SEQ], ALU.mult))
                    st.then(dve.tensor_tensor(slot(s)[:, SEQ:TOK], slot(s)[:, SEQ:TOK], slot(2 + s)[:, SEQ:TOK], ALU.mult))
                    st.wait()
                    dve.tensor_copy(us[:, :, HIST:HIST + STEPS], samp(slot(s)[:, SEQ:TOK])).then_inc(S.u_done, 1)
                    hold(dve, S.u_done, c + 3)
                    st.close()

                def convolve(c, s):
                    u = u_pad[s]
                    d = d_t[:, ds(c, 1), :].rearrange("p a n -> p (a n)")
                    w = cw[:, ds(c, 1), :].rearrange("p a k -> p (a k)")
                    b = par[:, ds(c + R_CB, 1)]
                    for t0 in (0, SEQ // 2):
                        st.then(dve.tensor_scalar(d[:, t0:t0 + SEQ // 2], u[:, t0:t0 + SEQ // 2], w[:, 0:1], b, ALU.mult, ALU.add))
                    for k in range(1, TAPS):
                        for t0 in (0, SEQ // 2):
                            dp = d[:, t0:t0 + SEQ // 2]
                            st.wait(back=1)
                            st.then(dve.scalar_tensor_tensor(out=dp, in0=u[:, t0 + k:t0 + k + SEQ // 2], scalar=w[:, k:k + 1], in1=dp,
                                                             op0=ALU.mult, op1=ALU.add))
                    st.close()

                with dve.Fori(0, 3) as cc:
                    for s in range(2):
                        make_u(cc * 2 + s, s)
                        convolve(cc * 2 + s, s)
                make_u(6, 0)
                make_u(7, 1)
                convolve(6, 0)
                convolve(7, 1)
                us_all = x_t[:, 0:CT_ * UW].rearrange("p (c b k) -> p c b k", c=CT_, b=SEQS)
                dd = d_t[:, :, SEQ:TOK].rearrange("p c (b t) -> p c b t", t=STEPS)

                def wide(ap):
                    return ap.unsqueeze(2).unsqueeze(3).to_broadcast([P, CT_, SEQS, STEPS])

                def term(k):
                    place = stg[:, 6 * TOK + 256 * (k % 3):6 * TOK + 256 * (k % 3) + 256].rearrange("p (c b t) -> p c b t", c=CT_, b=SEQS)
                    st.then(dve.tensor_tensor(place, us_all[:, :, :, k:k + STEPS], wide(cw[:, :, k]), ALU.mult))
                    return place

                sum_in = term(0)
                for k in range(TAPS):
                    place = sum_in
                    if k + 1 < TAPS:
                        sum_in = term(k + 1)
                    st.wait(back=1 if k + 1 < TAPS else 0)
                    st.then(dve.tensor_tensor(dd, place, wide(par[:, R_CB:R_CB + CT_]) if k == 0 else dd, ALU.add))
                st.close()
                st.then(dve.tensor_tensor(slot(7), d_t[:, 0, :], d_t[:, 1, :], ALU.add))
                for j in range(2, CT_):
                    st.wait()
                    ins = dve.tensor_tensor(slot(7), slot(7), d_t[:, j, :], ALU.add)
                    st.then(ins) if j < CT_ - 1 else ins.then_inc(S.mean_in, 1)
                st.close()

                def best(work, scores, m8, rounds, first=False):
                    if first:
                        st.then(dve.max(m8, scores))
                        st.wait()
                        st.then(dve.match_replace(work, m8, scores, NEG))
                        st.close()
                    with dve.Fori(0, rounds) as _r:
                        st.then(dve.max(m8, work))
                        st.wait()
                        st.then(dve.match_replace(work, m8, work, NEG))
                        st.close()

                def as_bias(work, scores):
                    st.then(dve.tensor_tensor(scores, work, scores, ALU.is_equal))
                    st.wait()
                    st.then(dve.tensor_scalar(scores, scores, -BIG, None, ALU.mult))

                dve.wait_ge(S.q_spilled, 16)
                for qt in range(1, QT):
                    sl = slice(qoff[qt], qoff[qt] + P * (qt + 1))
                    best(work_p[:, sl], bias_p[:, sl], top8[:, :], TOPK_P // 8 - 1, first=True)
                    as_bias(work_p[:, sl], bias_p[:, sl])
                st.close()
                dve.wait_ge(S.mean_done, 1)
                for j in range(CT_):
                    dve.tensor_tensor(d_t[:, j, :], d_t[:, j, :], slot(2), ALU.subtract).then_inc(S.cent_done, 1)
                for j in range(CT_):
                    dve.wait_ge(S.csq_done, j + 1)
                    if j == 0:
                        dve.tensor_copy(slot(6), slot(4)).then_inc(S.cvar_in, 1)
                    else:
                        dve.wait_ge(S.cvar_in, j)
                        dve.tensor_tensor(slot(6), slot(6), slot(4 + j % 2), ALU.add).then_inc(S.cvar_in, 1)
                best(work_s, bias_s, top8[0:NS, :], 9, first=True)
                dve.wait_ge(S.cstd_done, 1)
                st.then(dve.reciprocal(slot(3), slot(3)))
                st.close()
                for j in range(CT_):
                    dve.tensor_tensor(d_t[:, j, :], d_t[:, j, :], slot(3), ALU.mult).then_inc(S.ln_done, 1)
                best(work_s, bias_s, top8[0:NS, :], TOPK_S // 8 - 10)
                as_bias(work_s, bias_s)
                st.close()
                st.then(dve.tensor_copy(bias_p[:, 0:P], tab[:, T_TRIB:T_TRIB + P]))
                st.wait()
                dve.sem_inc(S.bias_done, 1)
                st.close()
                dve.wait_ge(S.silu_done, CT_)
                with dve.Fori(0, 4) as c:
                    for m in range(2):
                        d = d_t[:, ds(c * 2 + m, 1), :].rearrange("p a n -> p (a n)")
                        hold(dve, acc_free[m], c + (G_GC - G_IN + 2))
                        dve.tensor_tensor(d, d, slot(m), ALU.mult).then_inc(S.gc_done, 1)

                dve.wait_ge(S.gc_done, 2 + 8)
                for u in range(8):
                    qt, g = divmod(u, KVH)
                    n = P * (qt + 1)
                    dve.wait_ge(S.logits_p, u + 1)
                    if u >= 2:
                        f = sum(v // 2 + 1 for v in range(u - 1))
                        dve.wait_ge(S.ptr_p, f)
                    bias = bias_p[:, qoff[qt]:qoff[qt] + n]
                    for h in range(GROUP):
                        ins = dve.tensor_tensor_reduce(out=probs_p[:, u % 2, h, 0:n], in0=acc[:, h, 0:n], in1=bias, scale=HD ** -0.5,
                                                       scalar=NEG, op0=ALU.add, op1=ALU.max, accum_out=stat[:, h:h + 1])
                    ins.then_inc(S.probs_raw, 1)
                    dve.wait_ge(S.probs_raw, u + 1)
                    dve.tensor_scalar(stat[:, 4:8], stat[:, 0:4], -1.0, None, ALU.mult).then_inc(S.ppeak_done, 1)
                    dve.wait_ge(S.exp_p, u + 1)
                    st.then(dve.reciprocal(stat[:, 12:16], stat[:, 8:12]))
                    st.close()
                    for h in range(GROUP):
                        ins = dve.tensor_scalar(probs_p[:, u % 2, h, 0:n], probs_p[:, u % 2, h, 0:n], stat[:, 12 + h:13 + h], None, ALU.mult)
                    ins.then_inc(S.p_ready, 1)
                    if u >= 1:
                        qb, gb = divmod(u - 1, KVH)
                        dve.wait_ge(S.ptc_p, sum(v // 2 + 1 for v in range(u)))
                        dve.tensor_copy(attn_o[:, GROUP * gb:GROUP * gb + GROUP, qb * P:qb * P + P],
                                        aux[:, 2 + (u - 1) % 2, :].rearrange("p (h n) -> p h n", h=GROUP)).then_inc(S.ao_p, 1)
                dve.wait_ge(S.ptc_p, 20)
                dve.tensor_copy(attn_o[:, GROUP:HEADS, 3 * P:4 * P], aux[:, 3, :].rearrange("p (h n) -> p h n", h=GROUP)).then_inc(S.ao_p, 1)

                dve.sem_inc(S.sraw_done, 1)
                dve.sem_inc(S.k_cp_b, 1)
                dve.sem_inc(S.k_cp_a, 1)
                st.then(dve.memset(q_one[:, :, :], 0.0))
                st.close()

                def new_keys(b):
                    for g in range(KVH):
                        st.then(dve.tensor_copy(q_one[:, g, 16 * g:16 * g + 16].rearrange("p (j t) -> p j t", t=STEPS),
                                                q_att[:, GROUP * g:GROUP * g + GROUP, ds(b * STEPS + SEQ, STEPS)]))
                    dve.tensor_copy(k_turned[:, :, PAST:NKEY], k_new[:, :, ds(b * STEPS + SEQ, STEPS)]).then_inc(S.q_one_done, 1)
                    st.close()

                def k_copies(b, fs):
                    for f in fs:
                        hold(dve, S.k_turn_b, b * 4 + (4 + f // 2 + 1))
                        dve.tensor_copy(k_turned[:, f // 4, (f % 4) * 512:(f % 4) * 512 + 512], aux[:, 2, :]).then_inc(S.k_cp_b, 1)

                def soft1(b):
                    hold(dve, S.logits_s, b + 1)
                    hold(dve, S.brep_in, b * 128 + 128)
                    st.then(dve.tensor_tensor_reduce(out=probs_s[:, 0:PAST], in0=acc[0:NS, :, :].rearrange("p c n -> p (c n)"),
                                                     in1=bias_rep[:, 0:PAST], scale=HD ** -0.5, scalar=NEG, op0=ALU.add, op1=ALU.max,
                                                     accum_out=stat[0:NS, 0:1]))
                    st.then(dve.tensor_tensor_reduce(out=probs_s[:, PAST:NKEY], in0=aux[0:NS, 0, 0:STEPS], in1=bias_rep[:, PAST:NKEY],
                                                     scale=HD ** -0.5, scalar=NEG, op0=ALU.add, op1=ALU.max, accum_out=stat[0:NS, 3:4]))
                    st.close()
                    dve.tensor_scalar(stat[0:NS, 1:2], stat[0:NS, 0:1], stat[0:NS, 3:4], -1.0, ALU.max, ALU.mult).then_inc(S.sraw_done, 1)

                def soft2(b):
                    hold(dve, S.exp_s, b + 1)
                    st.then(dve.reciprocal(stat[0:NS, 12:13], stat[0:NS, 2:3]))
                    st.then(dve.memset(p_tail, 0.0))
                    st.wait()
                    st.then(dve.tensor_scalar(probs_s, probs_s, stat[0:NS, 12:13], None, ALU.mult))
                    st.close()
                    dve.tensor_copy(p_tail[:, ds(b * STEPS, STEPS)], probs_s[:, PAST:NKEY]).then_inc(S.ps_ready, 1)

                def soft3(b):
                    hold(dve, S.pts_ps, b + 1)
                    st.then(dve.tensor_copy(p_turned[:, 0:PAGES, :].rearrange("p k n -> p (k n)"), aux[:, 1, :]))
                    dve.tensor_copy(p_turned[0:NS, PAGES, :], aux[0:NS, 2, 0:NS]).then_inc(S.pts_done, 1)
                    st.close()
                    hold(dve, S.pv_s, b + 2)
                    dve.tensor_copy(attn_o[:, 0:HEADS, ds(b * STEPS + SEQ, STEPS)],
                                    aux[:, 3, 0:32].rearrange("p (h t) -> p h t", t=STEPS)).then_inc(S.ao_s, 1)

                new_keys(0)
                k_copies(0, (1, 3, 5, 7))
                with dve.Fori(0, SEQS - 1) as b:
                    soft1(b)
                    new_keys(b + 1)
                    k_copies(b + 1, (1, 3))
                    soft2(b)
                    k_copies(b + 1, (5, 7))
                    soft3(b)
                soft1(SEQS - 1)
                soft2(SEQS - 1)
                soft3(SEQS - 1)

                for n in range(8):
                    dve.wait_ge(S.split_hi, n + 1)
                    dve.tensor_tensor(act_hi[:, 8 + n, :], d_t[:, n, :], act_hi[:, n, :].bitcast(F32), ALU.subtract).then_inc(S.split_lo, 1)
                def rest_of(h):
                    dve.wait_ge(S.split_hi, 8 + h + 1)
                    dve.tensor_tensor(act_lo[:, 8 + h, :], slot(4 + h % 4), act_lo[:, h, :].bitcast(F32), ALU.subtract).then_inc(S.split_lo, 1)

                for h in range(HEADS):
                    dve.wait_ge(ga_in[h % 4], 16 * (h // 4 + 1))
                    if h >= 4:
                        dve.wait_ge(S.split_lo, 8 + h - 3)
                    dve.wait_ge(S.ao_s, 8)
                    dve.tensor_tensor(slot(4 + h % 4), attn_o[:, h, :], slot(h % 4), ALU.mult).then_inc(S.ag_ready, 1)
                    if h >= 1:
                        rest_of(h - 1)
                rest_of(HEADS - 1)

                dve.sem_inc(S.gates_used, 2)
                with dve.Fori(0, 4) as cc:
                    for s in range(2):
                        c = cc * 2 + s
                        g = G_MG + c
                        hold(dve, gates_in[s], cc * 32 + 32)
                        hold(dve, S.acc0_ready, c * 2 + (43 + 1))
                        dve.tensor_tensor(pair(xtile(c * 2)), accv(0), pair(slot(4 * s)), ALU.mult).then_inc(acc_free[0], 1)
                        hold(dve, S.w_used, 4 * g + (2 + 2))
                        dve.tensor_tensor(pair(xtile(c * 2 + 1)), accv(1), pair(slot(4 * s + 1)), ALU.mult).then_inc(acc_free[1], 1)
                        hold(dve, S.acc0_ready, c * 2 + (43 + 2))
                        dve.tensor_tensor(pair(slot(4 * s + 2)), accv(0), pair(slot(4 * s + 2)), ALU.mult).then_inc(acc_free[0], 1)
                        hold(dve, acc_free[0], c * 2 + (43 + 2 + 1))
                        st.then(dve.tensor_tensor(xtile(c * 2), xtile(c * 2), slot(4 * s + 2), ALU.add))
                        hold(dve, S.w_used, 4 * g + (4 + 2))
                        dve.tensor_tensor(pair(slot(4 * s + 3)), accv(1), pair(slot(4 * s + 3)), ALU.mult).then_inc(acc_free[1], 1)
                        hold(dve, acc_free[1], c * 2 + (43 + 2 + 1))
                        st.close()
                        dve.tensor_tensor(xtile(c * 2 + 1), xtile(c * 2 + 1), slot(4 * s + 3), ALU.add).then_inc(S.gates_used, 1)

                dve.sem_inc(S.x_new_done, 4)
                for k in range(KT):
                    dve.wait_ge(S.merged_hi, k + 1)
                    dve.tensor_tensor(act_lo[:, k, :], xtile(k), act_hi[:, k, :].bitcast(F32), ALU.subtract).then_inc(S.merged_lo, 1)
                with dve.Fori(0, 4) as cc:
                    for s in range(2):
                        c = cc * 2 + s
                        g = G_OUT + c
                        hold(dve, x_old_in[s], cc * 16 + 16)
                        for m in range(2):
                            if m == 0:
                                hold(dve, S.acc0_ready, c + (59 + 1))
                            else:
                                hold(dve, S.w_used, 4 * g + 6)
                            k = c * 2 + m
                            gate = mod[:, ds(k + 32, 1), :].rearrange("p a n -> p (a n)")
                            old = slot(2 * s + m)
                            st.then(dve.scalar_tensor_tensor(out=pair(xtile(k)), in0=accv(m), scalar=gate[:, 0:1], in1=pair(old),
                                                             op0=ALU.mult, op1=ALU.add))
                            dve.tensor_tensor(samp(slot(4 + 2 * s + m)[:, 0:NS]), samp(acc[:, 2 * m + 1, HALF - NS:HALF]), bc(gate[:, 1:9], STEPS),
                                              ALU.mult).then_inc(acc_free[m], 1)
                            hold(dve, acc_free[m], c + (59 + 2))
                            st.close()
                            xs = x_t[:, ds(k * TOK + SEQ, NS)]
                            dve.tensor_tensor(xs, slot(4 + 2 * s + m)[:, 0:NS], old[:, SEQ:TOK], ALU.add).then_inc(S.x_new_done, 1)
                end_of_layer(dve, l + 2)


_INS = ['x_prompt', 'x_sample', 'c_prompt', 'c_sample', 'cache_k', 'cache_v', 'cache_kidx', 'state_conv', 'page_table',
        'norm_g', 'w_ada', 'b_ada', 'w_in', 'q_norm_g', 'k_norm_g', 'idx_k_norm_g', 'conv_w', 'conv_b', 'conv_ln_g',
        'conv_ln_b', 'w_attn_out', 'w_conv_out', 'w_out']
_OUTS = [(1, SEQ, DM), (SEQS, STEPS, DM), (DEPTH, 1, SEQ, KVH, HD), (DEPTH, 1, SEQ, KVH, HD), (DEPTH, 1, SEQ, ID),
         (DEPTH, 1, HIST, CW_), (DEPTH, SEQS, STEPS, KVH, HD), (DEPTH, SEQS, STEPS, KVH, HD), (DEPTH, SEQS, STEPS, ID),
         (DEPTH, SEQS, HIST, CW_)]


def kernel(**inputs):
    import numpy as _np
    import concourse.bacc as _bacc
    from concourse import mybir as _mybir
    from concourse.bass_utils import run_bass_kernel_spmd as _run

    nc = _bacc.Bacc("TRN2", target_bir_lowering=False, num_devices=1)
    arrays, args = {}, []
    for name in _INS:
        a = _np.ascontiguousarray(inputs[name])
        arrays[f"in_{name}_dram"] = a
        args.append(nc.dram_tensor(f"in_{name}_dram", a.shape, _mybir.dt.from_np(a.dtype), kind="ExternalInput").ap())
    t = tables()
    arrays["in_table_dram"] = t
    args.append(nc.dram_tensor("in_table_dram", t.shape, _mybir.dt.from_np(t.dtype), kind="ExternalInput").ap())
    for i, shape in enumerate(_OUTS):
        args.append(nc.dram_tensor(f"out_{i}_dram", shape, _mybir.dt.float32, kind="ExternalOutput").ap())
    trunk_kernel(nc, *args)
    r = _run(nc, [arrays], core_ids=[0])
    return tuple(r.results[0][f"out_{i}_dram"] for i in range(len(_OUTS)))
```
